# Optimizing a Trainium2 kernel written in Bass

```python
import jax, jax.numpy as jnp
from jax import lax
import numpy as np

D_MODEL = 2048
BATCH = 1
SEQ = 256
DEPTH = 2

D_MIX = D_MODEL
HEAD_DIM = 128
ATTN_WIDTH = D_MIX // 2
N_ATTN_HEADS = ATTN_WIDTH // HEAD_DIM
GMLP_WIDTH = D_MIX // 4
N_GMLP_HEADS = 4
GMLP_HEAD_DIM = GMLP_WIDTH // N_GMLP_HEADS
POOL_WIDTH = D_MIX - ATTN_WIDTH - GMLP_WIDTH
N_POOL_GROUPS = 4
POOL_GROUP_DIM = POOL_WIDTH // N_POOL_GROUPS
POOL_WINDOWS = (2, 4, 8, 16)
CHUNK = 128
Q_BLOCK = 128
D_PLE = 256
D_FF = -(-8 * D_MODEL // (3 * 256)) * 256
EPS = 1e-6

PROJ_SIZES = (ATTN_WIDTH, ATTN_WIDTH, ATTN_WIDTH, N_ATTN_HEADS, GMLP_WIDTH, GMLP_WIDTH, POOL_WIDTH)
D_PROJ = 3 * ATTN_WIDTH + N_ATTN_HEADS + 2 * GMLP_WIDTH + POOL_WIDTH
SPLIT_POINTS = (
    ATTN_WIDTH,
    2 * ATTN_WIDTH,
    3 * ATTN_WIDTH,
    3 * ATTN_WIDTH + N_ATTN_HEADS,
    3 * ATTN_WIDTH + N_ATTN_HEADS + GMLP_WIDTH,
    3 * ATTN_WIDTH + N_ATTN_HEADS + 2 * GMLP_WIDTH,
)

kernel_name = "hybrid_parallel_fox_gmlp_pool_block"

def rms_norm(x, gain):
    xf = x.astype(jnp.float32)
    y = xf * lax.rsqrt(jnp.mean(xf * xf, axis=-1, keepdims=True) + EPS)
    return (y * gain.astype(jnp.float32)).astype(x.dtype)

def fox_attention(q, k, v, log_f):
    B, S, H, Dh = q.shape
    nb = S // Q_BLOCK
    c = jnp.cumsum(log_f, axis=1)
    q_blocks = q.reshape(B, nb, Q_BLOCK, H, Dh).transpose(1, 0, 3, 2, 4)
    cq_blocks = c.reshape(B, nb, Q_BLOCK, H).transpose(1, 0, 3, 2)
    pos_blocks = jnp.arange(S, dtype=jnp.int32).reshape(nb, Q_BLOCK)
    kh = k.transpose(0, 2, 1, 3)
    vh = v.transpose(0, 2, 1, 3)
    ck = c.transpose(0, 2, 1)
    kpos = jnp.arange(S, dtype=jnp.int32)
    scale = Dh ** -0.5

    def one_block(args):
        q_blk, cq_blk, qpos = args
        s = jnp.einsum('bhqd,bhkd->bhqk', q_blk, kh, preferred_element_type=jnp.float32) * scale
        s = s + (cq_blk[..., :, None] - ck[:, :, None, :])
        s = jnp.where(qpos[:, None] >= kpos[None, :], s, -jnp.inf)
        w = jax.nn.softmax(s, axis=-1)
        return jnp.einsum('bhqk,bhkd->bhqd', w.astype(vh.dtype), vh)

    out = lax.map(one_block, (q_blocks, cq_blocks, pos_blocks))
    return out.transpose(1, 0, 3, 2, 4).reshape(B, S, H * Dh)

def gmlp_mixer(u, v, v_gain, w_s, b_s):
    B, S, _ = u.shape
    nc = S // CHUNK
    u = jax.nn.gelu(u)
    v = jax.nn.gelu(v).reshape(B, S, N_GMLP_HEADS, GMLP_HEAD_DIM)
    v = rms_norm(v, v_gain).reshape(B, nc, CHUNK, N_GMLP_HEADS, GMLP_HEAD_DIM)
    w = w_s * jnp.tril(jnp.ones((CHUNK, CHUNK), w_s.dtype))[None]
    mixed = jnp.einsum('gts,bnsgc->bntgc', w, v) + b_s.T[None, None, :, :, None]
    return u * mixed.reshape(B, S, GMLP_WIDTH)

def pool_mixer(xp, w_pool, scale):
    B, S, _ = xp.shape
    x4 = xp.reshape(B, S, N_POOL_GROUPS, POOL_GROUP_DIM)
    cs = jnp.cumsum(x4.astype(jnp.float32), axis=1)
    cpad = jnp.concatenate([jnp.zeros((B, 1, N_POOL_GROUPS, POOL_GROUP_DIM), jnp.float32), cs], axis=1)
    t = jnp.arange(S, dtype=jnp.int32)[:, None]
    win = jnp.asarray(POOL_WINDOWS, dtype=jnp.int32)[None, :]
    lo = jnp.maximum(t + 1 - win, 0)
    cnt = (t + 1 - lo).astype(jnp.float32)
    g_idx = jnp.arange(N_POOL_GROUPS, dtype=jnp.int32)[None, :]
    window_sum = cs - cpad[:, lo, g_idx, :]
    d = (window_sum / cnt[None, :, :, None] - x4.astype(jnp.float32)).astype(xp.dtype)
    y = jnp.einsum('bsgc,gcd->bsgd', d, w_pool)
    return y.reshape(B, S, POOL_WIDTH) * scale

def setup_inputs(seed: int = 0) -> dict:
    key = jax.random.key(seed)
    ks = jax.random.split(key, 20)
    f32 = jnp.float32

    def nrm(k, shape, s):
        return jax.random.normal(k, shape, f32) * s

    def gain(k, shape):
        return 1.0 + 0.05 * jax.random.normal(k, shape, f32)

    return {
        "x": jax.random.normal(ks[0], (BATCH, SEQ, D_MODEL), f32),
        "p": jax.random.normal(ks[1], (DEPTH, BATCH, SEQ, D_PLE), f32),
        "norm_mix": gain(ks[2], (DEPTH, D_MODEL)),
        "w_in": nrm(ks[3], (DEPTH, D_MODEL, D_PROJ), D_MODEL ** -0.5),
        "q_norm": gain(ks[4], (DEPTH, HEAD_DIM)),
        "k_norm": gain(ks[5], (DEPTH, HEAD_DIM)),
        "forget_bias": 3.0 + 0.5 * jax.random.normal(ks[6], (DEPTH, N_ATTN_HEADS), f32),
        "gmlp_v_norm": gain(ks[7], (DEPTH, N_GMLP_HEADS, GMLP_HEAD_DIM)),
        "gmlp_w_s": nrm(ks[8], (DEPTH, N_GMLP_HEADS, CHUNK, CHUNK), CHUNK ** -0.5),
        "gmlp_b_s": 1.0 + 0.1 * jax.random.normal(ks[9], (DEPTH, N_GMLP_HEADS, CHUNK), f32),
        "pool_w": nrm(ks[10], (DEPTH, N_POOL_GROUPS, POOL_GROUP_DIM, POOL_GROUP_DIM), POOL_GROUP_DIM ** -0.5),
        "pool_scale": 1.0 + 0.1 * jax.random.normal(ks[11], (DEPTH, POOL_WIDTH), f32),
        "w_out": nrm(ks[12], (DEPTH, D_MIX, D_MODEL), D_MIX ** -0.5),
        "norm_ffn": gain(ks[13], (DEPTH, D_MODEL)),
        "w_ffn_gate": nrm(ks[14], (DEPTH, D_MODEL, D_FF), D_MODEL ** -0.5),
        "w_ffn_up": nrm(ks[15], (DEPTH, D_MODEL, D_FF), D_MODEL ** -0.5),
        "w_ffn_down": nrm(ks[16], (DEPTH, D_FF, D_MODEL), D_FF ** -0.5),
        "norm_ple": gain(ks[17], (DEPTH, D_MODEL)),
        "w_ple_gate": nrm(ks[18], (DEPTH, D_MODEL, D_MODEL), D_MODEL ** -0.5),
        "w_ple_proj": nrm(ks[19], (DEPTH, D_PLE, D_MODEL), D_PLE ** -0.5),
    }

def reference(x, p, norm_mix, w_in, q_norm, k_norm, forget_bias, gmlp_v_norm, gmlp_w_s, gmlp_b_s,
              pool_w, pool_scale, w_out, norm_ffn, w_ffn_gate, w_ffn_up, w_ffn_down,
              norm_ple, w_ple_gate, w_ple_proj):
    B, S, _ = x.shape
    h = x
    for i in range(DEPTH):
        xn = rms_norm(h, norm_mix[i])
        proj = xn @ w_in[i]
        q, k, v, f_logit, gu, gv, xp = jnp.split(proj, SPLIT_POINTS, axis=-1)
        q = rms_norm(q.reshape(B, S, N_ATTN_HEADS, HEAD_DIM), q_norm[i])
        k = rms_norm(k.reshape(B, S, N_ATTN_HEADS, HEAD_DIM), k_norm[i])
        v = v.reshape(B, S, N_ATTN_HEADS, HEAD_DIM)
        log_f = jax.nn.log_sigmoid((f_logit + forget_bias[i]).astype(jnp.float32))
        y_attn = fox_attention(q, k, v, log_f)
        y_gmlp = gmlp_mixer(gu, gv, gmlp_v_norm[i], gmlp_w_s[i], gmlp_b_s[i])
        y_pool = pool_mixer(xp, pool_w[i], pool_scale[i])
        mix = jnp.concatenate([y_attn, y_gmlp, y_pool], axis=-1)
        h = h + mix @ w_out[i]
        xn = rms_norm(h, norm_ffn[i])
        h = h + (jax.nn.silu(xn @ w_ffn_gate[i]) * (xn @ w_ffn_up[i])) @ w_ffn_down[i]
        gate = jax.nn.sigmoid(rms_norm(h, norm_ple[i]) @ w_ple_gate[i])
        h = h + (p[i] @ w_ple_proj[i]) * gate
    return h


_drawn_inputs = setup_inputs


def setup_inputs(seed=0):
    import zlib

    import numpy as np

    out = dict(_drawn_inputs(seed))
    spreads = {}
    factors = {'q_norm': 5.924, 'k_norm': 5.512, 'gmlp_v_norm': 4.371, 'norm_ple': 5.873}
    for name, (base, spread) in spreads.items():
        noise = np.random.default_rng([zlib.crc32(name.encode()), seed]).standard_normal(out[name].shape)
        drawn = base * np.exp(spread * noise) if base else spread * noise
        out[name] = __import__('jax').numpy.asarray(drawn.astype(out[name].dtype))
    for name, factor in factors.items():
        out[name] = (out[name] * factor).astype(out[name].dtype)
    return out
```

```python
from contextlib import ExitStack

import numpy as np

import concourse.bass as bass
from concourse import mybir

F32 = mybir.dt.float32
F32R = mybir.dt.float32r
ALU = mybir.AluOpType
ACT = mybir.ActivationFunctionType
AX_X = mybir.AxisListType.X

P = 128
COLS = 512
GK = 2
RING = 4
LEAD = 3
SEQ = 256
TB = SEQ // P
D = 2048
KT = D // P
D_FF = 5632
FKT = D_FF // P
HD = 128
HEADS = 8
HALF = HEADS // 2
ATTN = HEADS * HD
GRP = 4
MIXW = GRP * P
D_PLE = 256
DEPTH = 2
EPS = 1e-6
SCALE = float(HD) ** -0.5
MASKED = -1e38
WINDOWS = (2, 4, 8, 16)

F_COL = 3 * ATTN
GU_COL = F_COL + HEADS
GV_COL = GU_COL + MIXW
XP_COL = GV_COL + MIXW
IN_COLS = [0, ATTN, 2 * ATTN, COLS, ATTN + COLS, 2 * ATTN + COLS, XP_COL, GU_COL, GV_COL]
NG = KT // GK
NGD = FKT // GK
N_IN, N_OUT, N_FF, N_DN, N_PJ, N_PL = 9, D // COLS, D_FF // COLS, D // COLS, D // COLS, D // COLS
G_OUT = N_IN * NG
G_FF = G_OUT + N_OUT * NG
G_DN = G_FF + 2 * N_FF * NG
G_PJ = G_DN + N_DN * NGD
G_PL = G_PJ + N_PJ
GROUPS = G_PL + N_PL * NG
OUT_ORDER = [0, 1, 2, 3, 6, 7, 4, 5]
C_OUT = N_IN
C_FF = C_OUT + N_OUT
C_DN = C_FF + 2 * N_FF
C_PJ = C_DN + N_DN
C_PL = C_PJ + N_PJ
CHUNKS = C_PL + N_PL

TASKS = {"T1": 2, "T2": 2, "T3": 2, "EVQK": 0, "EVV": 0, "EVXP": 0, "EVGU": 0, "EVGV": 0, "TQK": 2,
         "WF": 0, "F": 0, "C": 1, "S": 1, "PT": 1, "PV": 1, "PT_P": 1, "PO1": 1, "PO2": 1, "WS": 1,
         "GM": 2, "GT": 2, "EVOUT": 0, "N": 0, "EVG": 0, "EVU": 0, "HT": 2, "EVPJ": 0, "EVPL": 0}


def make_plan():
    plan = {}

    def put(slot, kind, *args):
        plan.setdefault(slot, []).append((kind, *args))

    for c in range(3):
        put(-1, "T1", c)
    put(1, "T1", 3)
    put(3, "N", 0)
    put(5, "WF")
    for half in range(2):
        c0 = 3 * half
        put(NG * c0 + NG - 1, "EVQK", c0, half, 0)
        put(NG * c0 + NG + 2, "TQK", half, 0)
        put(NG * (c0 + 1) + NG - 1, "EVQK", c0 + 1, half, 1)
        put(NG * (c0 + 1) + NG + 2, "TQK", half, 1)
        put(NG * (c0 + 2) + NG - 1, "EVV", c0 + 2, half)
    put(2 * NG - 1, "F")
    put(2 * NG + 1, "C")
    put(2 * NG + 4, "PT_P")
    for h in range(HEADS):
        put(3 * NG + 6 * h, "S", h)
        put(3 * NG + 6 * h + 3, "PT", h)
        put(3 * NG + 6 * h + 5, "PV", h)
    put(7 * NG - 1, "EVXP", 6)
    for g in range(GRP):
        put(7 * NG + 1 + 2 * g, "PO1", g)
        put(7 * NG + 2 + 2 * g, "PO2", g)
    put(8 * NG - 1, "EVGU", 7)
    put(8 * NG + 2, "WS")
    put(9 * NG - 1, "EVGV", 8)
    put(G_OUT + 1, "GM")
    put(G_OUT + 3, "GT")
    for c in range(N_OUT):
        put(G_OUT + NG * c + NG - 1, "EVOUT", C_OUT + c, c)
        put(G_OUT + NG * (c + 1) + 1, "T2", c)
    put(G_FF + 3, "N", 1)
    put(G_PJ, "T3", 0)
    put(G_PJ, "T3", 1)
    put(G_PJ + 1, "T3", 2)
    put(G_PJ + 2, "T3", 3)
    for c in range(N_PJ):
        put(G_PJ + c, "EVPJ", C_PJ + c, c)
    put(G_PL + 2, "N", 2)
    for c in range(N_PL):
        put(G_PL + NG * c + NG - 1, "EVPL", C_PL + c, c)
    return plan


PLAN = make_plan()

AUX = 4
HT_BANKS = (0, 1)


def aux_uses():
    n = sum(TASKS[kind] for items in PLAN.values() for kind, *_ in items) + 2
    uses = [len(range(b, n, AUX)) for b in range(AUX)]
    for b in HT_BANKS:
        uses[b] += N_FF
    return uses


PER_LAYER = {"mm_done": GROUPS, "hi_ready": GROUPS, "lo_ready": GROUPS,
             "pair_free0": (CHUNKS + 1) // 2, "pair_free1": CHUNKS // 2,
             "norm_ready": 5, "gates_ready": 1, "probs_ready": HEADS, "h_ready": N_PL,
             "small_in": 6 * 16, "layer_start": 1, "wf_ready": 1, "raw": GROUPS // RING,
             "fn_ready": 106, "arg_ready": 20, "act_step": 10, "dve_step": 42}
for _b, _n in enumerate(aux_uses()):
    PER_LAYER[f"aux_full{_b}"] = PER_LAYER[f"aux_free{_b}"] = _n
PER_FF = {"mm_done": 2 * NG, "hi_ready": 2 * NG, "lo_ready": 2 * NG, "pair_free0": 1, "pair_free1": 1,
          "aux_full0": 1, "aux_full1": 1, "aux_free0": 1, "aux_free1": 1,
          "raw": 2 * NG // RING, "fn_ready": 2}
PER_DN = {"mm_done": 2 * NGD, "hi_ready": 2 * NGD, "lo_ready": 2 * NGD, "pair_free0": 1, "pair_free1": 1,
          "raw": 2 * NGD // RING}
CREDIT = {"h_ready": 1, "lo_ready": RING, "mm_done": RING, "pair_free0": 1, "pair_free1": 1,
          **{f"aux_free{b}": 1 for b in range(AUX)}}


class Counts:

    def __init__(self, names):
        self.n = {name: 0 for name in names}
        self.layer = 0
        self.loop = None

    def value(self, name, n=None):
        n = self.n[name] if n is None else n
        v = self.layer * PER_LAYER[name] + (CREDIT.get(name, 0) + n)
        if self.loop is not None:
            v = v + self.loop[0] * self.loop[1].get(name, 0)
        return v

    def add(self, name, k=1):
        self.n[name] += k

    def enter(self, register, step):
        self.loop, self.before = (register, step), dict(self.n)

    def leave(self, passes):
        for name, n in self.n.items():
            step = self.loop[1].get(name, 0)
            assert n - self.before[name] in (0, step), (name, n - self.before[name], step)
            if n != self.before[name]:
                self.n[name] = self.before[name] + passes * step
        self.loop = None

    def end_layer(self):
        off = {k: (n, PER_LAYER[k]) for k, n in self.n.items() if n and n != PER_LAYER[k]}
        assert not off, off


class Aux:

    def __init__(self, counts):
        self.counts, self.turn = counts, 0

    def take(self, bank=None):
        if bank is None:
            bank, self.turn = self.turn % AUX, self.turn + 1
        full, free = f"aux_full{bank}", f"aux_free{bank}"
        before = self.counts.value(free)
        self.counts.add(full)
        self.counts.add(free)
        return bank, before, self.counts.value(full), self.counts.value(free)


def trunk(nc, x, p, norm_mix, w_in, q_norm, k_norm, forget_bias, gmlp_v_norm, gmlp_w_s, gmlp_b_s, pool_w,
          pool_scale, w_out, norm_ffn, w_ffn_gate, w_ffn_up, w_ffn_down, norm_ple, w_ple_gate, w_ple_proj,
          consts, bands, out):
    with ExitStack() as ctx:
        def sb(name, shape, dt=F32):
            return ctx.enter_context(nc.sbuf_tensor(name, shape, dt))

        def sem(name):
            return ctx.enter_context(nc.semaphore(name))

        h = sb("h", [P, TB, D])
        raw = sb("raw", [P, RING, GK, COLS])
        w_hi = sb("w_hi", [P, RING, GK, COLS], F32R)
        w_lo = sb("w_lo", [P, RING, GK, COLS], F32R)
        BYTES = {"act_hi": FKT * SEQ * 4, "act_lo": FKT * SEQ * 4, "xn_hi": KT * SEQ * 4, "xn_lo": KT * SEQ * 4}
        OFFSET, at = {}, (nc.sbuf_base + 31) // 32 * 32
        sb("arena", [P, sum(BYTES.values()) // 4])
        for name, size in BYTES.items():
            OFFSET[name], at = at, at + size
        act_hi, act_lo, xn_hi, xn_lo = (nc.alloc_sbuf_tensor_at(
            name, [P, BYTES[name] // 4 // SEQ, SEQ], F32R, offset=OFFSET[name]) for name in BYTES)
        pt_hi = sb("pt_hi", [P, 2, SEQ], F32R)
        pt_lo = sb("pt_lo", [P, 2, SEQ], F32R)
        scratch = sb("scratch", [P, TB, COLS])
        work = sb("work", [P, TB, COLS])
        p_nat = sb("p_nat", [P, TB, D_PLE])
        const = sb("const", [P, 5 * P])
        gain_rows = scratch[:].rearrange("p t n -> p (t n)")[0:2 * 58, 0:P]
        gains = sb("gains", [P, 2 * 58])
        lg = sb("lg", [P, 58])
        f_bias = sb("f_bias", [P, DEPTH * HEADS])
        lf_bias = sb("lf_bias", [P, HEADS])
        wf = sb("wf", [P, KT, HEADS])
        wf_hi = sb("wf_hi", [P, KT, HEADS], F32R)
        wf_lo = sb("wf_lo", [P, KT, HEADS], F32R)
        w_st = sb("w_st", [P, GRP, P])
        stat = sb("stat", [P, 128])

        ident = const[:, 0:P]
        upper = const[:, P:2 * P]
        ones = const[:, 2 * P:3 * P]
        mask = const[:, 3 * P:5 * P]

        def over(name, host, first, shape):
            assert first + int(np.prod(shape[1:])) * 4 <= BYTES[host]
            return nc.alloc_sbuf_tensor_at(name, shape, F32, offset=OFFSET[host] + first)

        K = 1024
        v_nat = over("v_nat", "xn_hi", 0, [P, 2, TB, COLS])
        qk_nat = over("qk_nat", "xn_hi", 8 * K, [P, TB, COLS])
        probs_t = over("probs_t", "xn_hi", 12 * K, [P, 2, 3 * P])
        pool_d = over("pool_d", "xn_hi", 15 * K, [P, SEQ])
        q_t = over("q_t", "xn_lo", 0, [P, 2, HALF, SEQ])
        k_t = over("k_t", "xn_lo", 8 * K, [P, 2, HALF, SEQ])
        tail = 2 * KT * SEQ * 4
        gu = over("gu", "act_hi", tail, [P, TB, GRP, P])
        gv = over("gv", "act_hi", tail + 4 * K, [P, TB, GRP, P])
        xp = over("xp", "act_hi", tail + 8 * K, [P, TB, COLS])
        v_gain = over("v_gain", "act_lo", tail, [P, MIXW])
        w_s = over("w_s", "act_lo", tail + 2 * K, [P, GRP, P])
        w_pool = over("w_pool", "act_lo", tail + 4 * K, [P, GRP, P])
        band = over("band", "act_lo", tail + 6 * K, [P, GRP, 3, P])
        ple = over("ple", "act_lo", KT * SEQ * 4, [P, N_PJ, TB, COLS])

        ssq, var, rstd = stat[:, 0:4], stat[:, 4:6], stat[:, 6:12].rearrange("p (s t) -> p s t", s=3)
        dev = stat[:, 12:14]
        hss, hvar, hdev, hr = (stat[:, a:a + 8] for a in (16, 24, 32, 40))
        fstat = sb("fstat", [P, 6, TB, HEADS])
        z, nz, ef, lnf, logf, cum = (fstat[:, a] for a in range(6))
        neg_cum = sb("neg_cum", [HEADS, SEQ])
        mx, nmx, den, rden = (stat[:, a:a + 2] for a in (48, 50, 52, 54))

        acc = ctx.enter_context(nc.psum_tensor("acc", [P, 2, TB, COLS], F32))
        aux_ps = ctx.enter_context(nc.psum_tensor("aux_ps", [P, AUX, COLS], F32))

        raw_in = [sem(f"raw_in{i}") for i in range(RING)]
        x_in, start_in, small_in, out_sent = sem("x_in"), sem("start_in"), sem("small_in"), sem("out_sent")
        s = {name: sem(name) for name in PER_LAYER if name not in ("small_in", "raw")}
        s["small_in"] = small_in
        gains_t, gains_in = sem("gains_t"), sem("gains_in")
        names = list(PER_LAYER)

        h_of = lambda t: t.rearrange("b (t p) n -> p (b t) n", p=P)

        def group_of(w, layer, k, col, width=COLS):
            return w[bass.ds(layer, 1), bass.ds(k * (GK * P), GK * P), bass.ds(col, width)].rearrange(
                "l (j p) n -> p (l j) n", p=P)

        block = ctx.enter_context(nc.Block())

        @block.sync
        def _(sp):
            sp.sem_inc(s["lo_ready"], RING)
            c = Counts(names)

            def load(n, src):
                slot = n % RING
                sp.wait_ge(s["lo_ready"], c.value("lo_ready", n - RING + 1))
                sp.dma_start(raw[:, slot], src).then_inc(raw_in[slot], 16)

            with sp.Fori(0, DEPTH) as layer:
                c.layer = layer
                for i, col in enumerate(IN_COLS):
                    for k in range(NG):
                        load(i * NG + k, group_of(w_in, layer, k, col))
                with sp.Fori(0, N_OUT) as i:
                    c.loop = (i, {"lo_ready": NG})
                    for k in range(NG):
                        load(G_OUT + k, group_of(w_out, layer, OUT_ORDER[k], i * COLS))
                with sp.Fori(0, N_FF) as i:
                    c.loop = (i, PER_FF)
                    for half, w in enumerate((w_ffn_gate, w_ffn_up)):
                        for k in range(NG):
                            load(G_FF + half * NG + k, group_of(w, layer, k, i * COLS))
                with sp.Fori(0, N_DN // 2) as i:
                    c.loop = (i, PER_DN)
                    for m in range(2 * NGD):
                        load(G_DN + m, group_of(w_ffn_down, layer, m % NGD, i * (2 * COLS) + m // NGD * COLS))
                c.loop = None
                for i in range(N_PJ):
                    load(G_PJ + i, group_of(w_ple_proj, layer, 0, i * COLS))
                with sp.Fori(0, N_PL) as i:
                    c.loop = (i, {"lo_ready": NG})
                    for k in range(NG):
                        load(G_PL + k, group_of(w_ple_gate, layer, k, i * COLS))
                c.loop = None
            for i in range(N_PL):
                cols = slice(i * COLS, (i + 1) * COLS)
                sp.wait_ge(s["h_ready"], CREDIT["h_ready"] + (DEPTH - 1) * N_PL + i + 1)
                sp.dma_start(h_of(out)[:, :, cols], h[:, :, cols]).then_inc(out_sent, 16)
            sp.wait_ge(out_sent, 16 * N_PL)

        @block.gpsimd
        def _(pool):
            pool.dma_start(h[:], h_of(x)).then_inc(x_in, 16)
            pool.dma_start(const[:], consts).then_inc(start_in, 16)
            for layer in range(DEPTH):
                row = layer * 58
                for g, n in ((norm_mix, KT), (norm_ffn, KT), (norm_ple, KT), (q_norm, 1), (k_norm, 1),
                             (pool_scale, GRP)):
                    pool.dma_start(gain_rows[row:row + n, :], g[layer].rearrange("(k p) -> k p", p=P)
                                   ).then_inc(start_in, 16)
                    row += n
                pool.dma_start(gain_rows[row:row + GRP, :], gmlp_b_s[layer]).then_inc(start_in, 16)
            pool.dma_start(f_bias[:], forget_bias.rearrange("l h -> (l h)").partition_broadcast(P)
                           ).then_inc(start_in, 16)
            with pool.Fori(0, DEPTH) as layer:
                pool.wait_ge(s["mm_done"], layer * GROUPS + RING)
                for dst, src in (
                    (wf[:], w_in[bass.ds(layer, 1), :, F_COL:F_COL + HEADS].rearrange("l (k p) n -> p (l k) n", p=P)),
                    (p_nat[:], p[bass.ds(layer, 1)].rearrange("l b (t p) n -> p (l b t) n", p=P)),
                    (v_gain[:], gmlp_v_norm[bass.ds(layer, 1)].rearrange("l g c -> (l g c)").partition_broadcast(P)),
                    (w_s[:], gmlp_w_s[bass.ds(layer, 1)].rearrange("l g t s -> t (l g) s")),
                    (w_pool[:], pool_w[bass.ds(layer, 1)].rearrange("l g c d -> c (l g) d")),
                    (band[:], bands),
                ):
                    pool.dma_start(dst, src).then_inc(small_in, 16)

        @block.tensor
        def _(pe):
            c = Counts(names)
            for name in ("pair_free0", "pair_free1", *(f"aux_free{b}" for b in range(AUX))):
                pe.sem_inc(s[name], 1)
            done = {}

            def claim(task, *needs):
                evacuated(*(t for t in needs if t[0] != task[0]))
                pe.wait_ge(s[f"aux_free{task[0]}"], task[1])
                return aux_ps[:, task[0]]

            def evacuated(*tasks):
                for bank, value in {t[0]: t[3] for t in tasks}.items():
                    pe.wait_ge(s[f"aux_free{bank}"], value)

            def filled(ins, task):
                ins.then_inc(s[f"aux_full{task[0]}"], 1)

            def group(n, tiles, hi, lo, chunk, first, last, forget=None):
                slot = n % RING
                c.add("lo_ready")
                c.add("mm_done")
                pe.wait_ge(s["lo_ready"], c.value("lo_ready"))
                if first:
                    pe.wait_ge(s[f"pair_free{chunk % 2}"], c.value(f"pair_free{chunk % 2}"))
                for j, k in enumerate(tiles):
                    for t in range(TB):
                        ps = acc[:, chunk % 2, t, :]
                        x_hi, x_lo = (a[:, k, t * P:(t + 1) * P] for a in (hi, lo))
                        a = first and j == 0
                        z_ = last and j == len(tiles) - 1
                        pe.matmul(ps, x_hi, w_hi[:, slot, j, :], start=a, stop=False)
                        pe.matmul(ps, x_hi, w_lo[:, slot, j, :], start=False, stop=False)
                        if forget:
                            fo = aux_ps[:, forget[t][0], 0:HEADS]
                            pe.matmul(fo, x_hi, wf_hi[:, k, :], start=a, stop=False)
                            pe.matmul(fo, x_hi, wf_lo[:, k, :], start=False, stop=False)
                            f = pe.matmul(fo, x_lo, wf_hi[:, k, :], start=False, stop=z_)
                            if z_:
                                filled(f, forget[t])
                        mm = pe.matmul(ps, x_lo, w_hi[:, slot, j, :], start=False, stop=z_)
                mm.then_inc(s["mm_done"], 1)

            def turn(task, blocks, *needs):
                bank = claim(task, *needs)
                for i, b in enumerate(blocks):
                    t = pe.transpose(bank[:, i * P:(i + 1) * P], b, ident)
                filled(t, task)

            def turn_h(tasks, col):
                for a, task in enumerate(tasks):
                    turn(task, [h[:, t, (4 * col + 2 * a + j) * P:(4 * col + 2 * a + j + 1) * P]
                                for j in range(2) for t in range(TB)])

            def T1(tasks, col):
                if col == 0:
                    pe.wait_ge(s["h_ready"], c.value("h_ready", 0))
                turn_h(tasks, col)

            def T2(tasks, col):
                pair = f"pair_free{(C_OUT + col) % 2}"
                pe.wait_ge(s[pair], done[("h", C_OUT + col)])
                turn_h(tasks, col)

            def T3(tasks, col):
                if col == 0:
                    for pair in ("pair_free0", "pair_free1"):
                        pe.wait_ge(s[pair], done[("down", pair)])
                turn_h(tasks, col)

            def TQK(tasks, half, which):
                c.add("norm_ready")
                pe.wait_ge(s["norm_ready"], c.value("norm_ready"))
                for a, task in enumerate(tasks):
                    turn(task, [qk_nat[:, t, (2 * a + j) * P:(2 * a + j + 1) * P]
                                for j in range(2) for t in range(TB)])
                done[("qk", half, which)] = tasks

            def C(tasks):
                (task,) = tasks
                bank = claim(task)
                c.add("gates_ready")
                pe.wait_ge(s["gates_ready"], c.value("gates_ready"))
                pe.matmul(bank[:, 0:HEADS], upper, logf[:, 0], start=True, stop=True)
                pe.matmul(bank[:, HEADS:2 * HEADS], ones, logf[:, 0], start=True, stop=False)
                pe.matmul(bank[:, HEADS:2 * HEADS], upper, logf[:, 1], start=False, stop=True)
                row = bank[0:HEADS, P:P + SEQ]
                pe.matmul(row[:, 0:P], logf[:, 0], upper, start=True, stop=True)
                pe.matmul(row[:, P:SEQ], logf[:, 0], ones, start=True, stop=False)
                filled(pe.matmul(row[:, P:SEQ], logf[:, 1], upper, start=False, stop=True), task)
                done["c"] = task

            def S(tasks, hd):
                (task,) = tasks
                half, i = divmod(hd, HALF)
                needs = () if i else (done["c"], *done[("qk", half, 0)], *done[("qk", half, 1)])
                bank = claim(task, *needs)
                for t, keys in ((0, P), (1, SEQ)):
                    o = bank[:, t * SEQ:t * SEQ + keys]
                    pe.matmul(o, q_t[:, half, i, t * P:(t + 1) * P], k_t[:, half, i, 0:keys], start=True, stop=False)
                    mm = pe.matmul(o, ident[0:HEADS, hd:hd + 1].to_broadcast([HEADS, P]),
                                   neg_cum[:, 0:keys], start=False, stop=True)
                filled(mm, task)

            def PT(tasks, hd):
                c.add("probs_ready")
                pe.wait_ge(s["probs_ready"], c.value("probs_ready"))
                pr = work[:, hd % 2].rearrange("p (t k) -> p t k", t=TB)
                turn(tasks[0], [pr[:, 0, 0:P], pr[:, 1, 0:P], pr[:, 1, P:SEQ]])
                done[("pt", hd)] = tasks[0]

            def PV(tasks, hd):
                (task,) = tasks
                half, i = divmod(hd, HALF)
                if i == 0:
                    pe.wait_ge(s[f"pair_free{(3 * half + 2) % 2}"], done[("v", half)])
                bank = claim(task, done[("pt", hd)])
                cols = slice(i * HD, (i + 1) * HD)
                pt = probs_t[:, hd % 2]
                pe.matmul(bank[:, 0:SEQ], v_nat[:, half, 0, cols], pt[:, 0:SEQ], start=True, stop=False)
                filled(pe.matmul(bank[:, P:SEQ], v_nat[:, half, 1, cols], pt[:, SEQ:3 * P],
                                 start=False, stop=True), task)

            def PT_P(tasks):
                pe.wait_ge(s["small_in"], c.value("small_in", PER_LAYER["small_in"]))
                turn(tasks[0], [p_nat[:, t, j * P:(j + 1) * P] for j in range(2) for t in range(TB)])
                done["p"] = tasks[0]

            def PO1(tasks, g):
                (task,) = tasks
                if g == 0:
                    pe.wait_ge(s["pair_free0"], done["xp"])
                bank = claim(task)
                cols = slice(g * P, (g + 1) * P)
                pe.matmul(bank[:, 0:SEQ], xp[:, 0, cols], band[:, g, 0:2].rearrange("p a b -> p (a b)"),
                          start=True, stop=False)
                filled(pe.matmul(bank[:, P:SEQ], xp[:, 1, cols], band[:, g, 2], start=False, stop=True), task)
                done[("po", g)] = task

            def PO2(tasks, g):
                bank = claim(tasks[0], done[("po", g)])
                filled(pe.matmul(bank[:, 0:SEQ], w_pool[:, g], pool_d[:], start=True, stop=True), tasks[0])

            def WS(tasks):
                turn(tasks[0], [w_s[:, g] for g in range(GRP)])
                done["ws"] = tasks[0]

            def GM(tasks):
                c.add("norm_ready")
                pe.wait_ge(s["norm_ready"], c.value("norm_ready"))
                for t, task in enumerate(tasks):
                    bank = claim(task, done["ws"])
                    for g in range(GRP):
                        mm = pe.matmul(bank[:, g * P:(g + 1) * P], w_st[:, g], gv[:, t, g], start=True, stop=True)
                    filled(mm, task)
                done["gm"] = tasks

            def GT(tasks):
                for a, task in enumerate(tasks):
                    turn(task, [gu[:, t, 2 * a + j] for j in range(2) for t in range(TB)], *done["gm"])
                done["gt"] = tasks

            def HT(tasks):
                pe.wait_ge(s[f"pair_free{(C_FF + 1) % 2}"], c.value(f"pair_free{(C_FF + 1) % 2}"))
                for a, task in enumerate(tasks):
                    turn(task, [work[:, t, (2 * a + j) * P:(2 * a + j + 1) * P]
                                for j in range(2) for t in range(TB)])

            def ev(chunk):
                c.add(f"pair_free{chunk % 2}")
                return c.value(f"pair_free{chunk % 2}")

            def EVV(tasks, chunk, half):
                done[("v", half)] = ev(chunk)

            def EVXP(tasks, chunk):
                done["xp"] = ev(chunk)

            def EVOUT(tasks, chunk, col):
                done[("h", chunk)] = ev(chunk)

            def counted(tasks, chunk, *_):
                ev(chunk)

            def nothing(tasks, *_):
                pass

            do = {"T1": T1, "T2": T2, "T3": T3, "TQK": TQK, "C": C, "S": S, "PT": PT, "PV": PV, "PT_P": PT_P,
                  "PO1": PO1, "PO2": PO2, "WS": WS, "GM": GM, "GT": GT, "EVQK": counted, "EVV": EVV,
                  "EVXP": EVXP, "EVGU": counted, "EVGV": counted, "EVOUT": EVOUT, "EVPJ": counted,
                  "EVPL": counted, "N": nothing, "WF": nothing, "F": nothing}

            def items(slot):
                for kind, *args in PLAN.get(slot, ()):
                    tasks = [aux.take() for _ in range(TASKS[kind])]
                    do[kind](tasks, *args)
                    if kind in ("T1", "T2", "T3"):
                        done[(kind, args[0])] = tasks
                    if kind in ("PV", "PO2"):
                        done[(kind, args[0])] = tasks[0]

            def mix_ready(kk):
                if kk < HEADS // 2:
                    evacuated(*(done[("PV", hd)] for hd in (2 * kk, 2 * kk + 1)))
                elif kk < (HEADS + GRP) // 2:
                    evacuated(done["gt"][kk - HEADS // 2])
                else:
                    evacuated(*(done[("PO2", 2 * kk - HEADS - GRP + j)] for j in range(2)))

            def tiles_ready(kind, k):
                evacuated(done[(kind, k // 4)][k % 4 // 2])

            pe.wait_ge(start_in, 16 * 16)
            pe.transpose(aux_ps[:, 0, 0:2 * 58], gain_rows, ident[0:2 * 58, 0:2 * 58]).then_inc(gains_t, 1)
            pe.wait_ge(gains_in, 1)
            pe.wait_ge(x_in, 16)
            pe.sem_inc(s["h_ready"], 1)

            with pe.Fori(0, DEPTH) as layer:
                c.layer = layer
                c.n = {name: 0 for name in names}
                aux = Aux(c)
                items(-1)
                for i in range(N_IN):
                    forget = [aux.take() for _ in range(TB)] if i == 1 else None
                    for k in range(NG):
                        n = i * NG + k
                        if i == 0:
                            tiles_ready("T1", GK * k)
                        if i == 1 and k == 0:
                            for t in forget:
                                claim(t)
                            pe.wait_ge(s["wf_ready"], layer + 1)
                        group(n, [GK * k, GK * k + 1], act_hi, act_lo, i, k == 0, k == NG - 1, forget)
                        items(n)
                for i in range(N_OUT):
                    for k in range(NG):
                        n = G_OUT + i * NG + k
                        kk = OUT_ORDER[k]
                        if i == 0:
                            mix_ready(kk)
                        group(n, [KT + GK * kk, KT + GK * kk + 1], act_hi, act_lo, C_OUT + i,
                              k == 0, k == NG - 1)
                        items(n)

                def hidden(n0, peeled):
                    for half in range(2):
                        for k in range(NG):
                            n = n0 + half * NG + k
                            if peeled and half == 0:
                                tiles_ready("T2", GK * k)
                            group(n, [GK * k, GK * k + 1], xn_hi, xn_lo, C_FF + half, k == 0, k == NG - 1)
                            if peeled:
                                items(n)
                            elif half == 0 and k == 2:
                                HT([aux.take(b) for b in HT_BANKS])
                        ev(C_FF + half)

                hidden(G_FF, True)
                with pe.Fori(0, N_FF - 1) as i:
                    c.enter(i, PER_FF)
                    hidden(G_FF, False)
                c.leave(N_FF - 1)

                HT_last = [aux.take(b) for b in HT_BANKS]
                HT(HT_last)
                with pe.Fori(0, N_DN // 2) as i:
                    c.enter(i, PER_DN)
                    for m in range(2 * NGD):
                        k, chunk = m % NGD, C_DN + m // NGD
                        if m == 20:
                            pe.wait_ge(s["aux_free0"], HT_last[0][3])
                        if m == 21:
                            pe.wait_ge(s["aux_free1"], HT_last[1][3])
                        group(G_DN + m, [GK * k, GK * k + 1], act_hi, act_lo, chunk, k == 0, k == NGD - 1)
                        if k == NGD - 1:
                            ev(chunk)
                c.leave(N_DN // 2)
                for pair in ("pair_free0", "pair_free1"):
                    done[("down", pair)] = c.value(pair)
                evacuated(done["p"])
                for i in range(N_PJ):
                    group(G_PJ + i, [0, 1], pt_hi, pt_lo, C_PJ + i, True, True)
                    items(G_PJ + i)
                for i in range(N_PL):
                    for k in range(NG):
                        n = G_PL + i * NG + k
                        if i == 0:
                            tiles_ready("T3", GK * k)
                        group(n, [GK * k, GK * k + 1], xn_hi, xn_lo, C_PL + i, k == 0, k == NG - 1)
                        items(n)
                c.end_layer()

        @block.scalar
        def _(act):
            c = Counts(names)
            act.sem_inc(s["mm_done"], RING)

            def split_hi(n):
                slot = n % RING
                act.wait_ge(raw_in[slot], c.value("raw", n // RING + 1) * 16)
                act.wait_ge(s["mm_done"], c.value("mm_done", n - RING + 1))
                nc.scalar.activation(w_hi[:, slot], raw[:, slot], ACT.Copy).then_inc(s["hi_ready"], 1)

            def bank_full(task):
                act.wait_ge(s[f"aux_full{task[0]}"], task[2])
                return aux_ps[:, task[0]]

            def chunk_done(slot):
                act.wait_ge(s["mm_done"], c.value("mm_done", slot + 1))

            def answer(ins):
                ins.then_inc(s["fn_ready"], 1)
                c.add("fn_ready")

            def asked():
                c.add("arg_ready")
                act.wait_ge(s["arg_ready"], c.value("arg_ready"))

            def step(ins):
                ins.then_inc(s["act_step"], 1)
                c.add("act_step")
                act.wait_ge(s["act_step"], c.value("act_step"))

            def ev(chunk):
                c.add(f"pair_free{chunk % 2}")

            def out_of(chunk, slot, dst, func, stage):
                chunk_done(slot)
                for t in range(TB):
                    ins = nc.scalar.activation(dst[t], acc[:, chunk % 2, t, :], func, scale=rstd[:, stage, t:t + 1])
                ins.then_inc(s[f"pair_free{chunk % 2}"], 1)
                ev(chunk)

            def hi(bank, dst, gain=None):
                answer(nc.scalar.activation(dst, bank, ACT.Copy, scale=1.0 if gain is None else gain))

            def turned_h(tasks, col, dst, gain):
                for a, task in enumerate(tasks):
                    bank = bank_full(task)
                    for j in range(2):
                        k = 4 * col + 2 * a + j
                        hi(bank[:, j * SEQ:(j + 1) * SEQ], dst[:, k], lg[:, gain + k:gain + k + 1])

            def N(slot, tasks, stage):
                if stage == 0:
                    act.wait_ge(s["h_ready"], c.value("h_ready", 0))
                else:
                    for pair in ("pair_free0", "pair_free1"):
                        act.wait_ge(s[pair], c.value(pair))
                flat = scratch[:].rearrange("p t n -> p (t n)")
                for i in range(2 * TB):
                    t, half = divmod(i, 2)
                    ins = nc.scalar.activation(flat, h[:, t, half * D // 2:(half + 1) * D // 2], ACT.Square,
                                               accum_out=ssq[:, i:i + 1])
                    if i < 2 * TB - 1:
                        step(ins)
                answer(ins)
                asked()
                answer(nc.scalar.activation(dev, var, ACT.Sqrt))
                asked()

            def root():
                asked()
                answer(nc.scalar.activation(hdev, hvar, ACT.Sqrt))

            def EVQK(slot, tasks, chunk, half, which):
                if half or which:
                    for t in last_qk:
                        act.wait_ge(s[f"aux_free{t[0]}"], t[3])
                out_of(chunk, slot, [qk_nat[:, t] for t in range(TB)], ACT.Copy, 0)
                root()

            last_qk = []

            def TQK(slot, tasks, half, which):
                last_qk[:] = tasks

            def EVV(slot, tasks, chunk, half):
                out_of(chunk, slot, [v_nat[:, half, t] for t in range(TB)], ACT.Copy, 0)

            def EVXP(slot, tasks, chunk):
                out_of(chunk, slot, [xp[:, t] for t in range(TB)], ACT.Copy, 0)

            def flat_of(x4):
                return [x4[:, t].rearrange("p g c -> p (g c)") for t in range(TB)]

            def EVGU(slot, tasks, chunk):
                out_of(chunk, slot, flat_of(gu), ACT.Gelu_apprx_tanh, 0)

            def EVGV(slot, tasks, chunk):
                out_of(chunk, slot, flat_of(gv), ACT.Gelu_apprx_tanh, 0)
                root()

            def WF(slot, tasks):
                act.wait_ge(s["small_in"], c.value("small_in", PER_LAYER["small_in"]))
                answer(nc.scalar.activation(wf_hi[:], wf[:], ACT.Copy))

            def F(slot, tasks):
                asked()
                step(nc.scalar.activation(ef, nz, ACT.Exp))
                answer(nc.scalar.activation(lnf, ef, ACT.Ln, bias=1.0))

            def S(slot, tasks, hd):
                asked()
                pr = work[:, hd % 2].rearrange("p (t k) -> p t k", t=TB)
                for t, keys in ((0, P), (1, SEQ)):
                    ins = nc.scalar.activation(pr[:, t, 0:keys], pr[:, t, 0:keys], ACT.Exp,
                                               bias=nmx[:, t:t + 1], accum_out=den[:, t:t + 1])
                answer(ins)

            def PT(slot, tasks, hd):
                bank = bank_full(tasks[0])
                nc.scalar.activation(probs_t[:, hd % 2], bank[:, 0:3 * P], ACT.Copy
                                     ).then_inc(s[f"aux_free{tasks[0][0]}"], 1)

            def PV(slot, tasks, hd):
                hi(bank_full(tasks[0])[:, 0:SEQ], act_hi[:, KT + hd])

            def PT_P(slot, tasks):
                hi(bank_full(tasks[0])[:], pt_hi[:].rearrange("p k t -> p (k t)"))

            def PO1(slot, tasks, g):
                bank = bank_full(tasks[0])
                nc.scalar.activation(pool_d[:], bank[:, 0:SEQ], ACT.Copy).then_inc(s[f"aux_free{tasks[0][0]}"], 1)

            def PO2(slot, tasks, g):
                hi(bank_full(tasks[0])[:, 0:SEQ], act_hi[:, KT + HEADS + GRP + g], lg[:, 50 + g:51 + g])

            def GT(slot, tasks):
                for a, task in enumerate(tasks):
                    k = KT + HEADS + 2 * a
                    hi(bank_full(task)[:], act_hi[:, k:k + 2].rearrange("p k t -> p (k t)"))

            def T1(slot, tasks, col):
                turned_h(tasks, col, act_hi, 0)

            def T2(slot, tasks, col):
                turned_h(tasks, col, xn_hi, KT)

            def T3(slot, tasks, col):
                turned_h(tasks, col, xn_hi, 2 * KT)

            def EVOUT(slot, tasks, chunk, col):
                ev(chunk)

            def EVPJ(slot, tasks, chunk, col):
                chunk_done(slot)
                nc.scalar.activation(ple[:, col], acc[:, chunk % 2], ACT.Copy
                                     ).then_inc(s[f"pair_free{chunk % 2}"], 1)
                ev(chunk)

            def EVPL(slot, tasks, chunk, col):
                act.wait_ge(s["h_ready"], c.value("h_ready"))
                out_of(chunk, slot, [scratch[:, t] for t in range(TB)], ACT.Sigmoid, 2)
                c.add("h_ready")

            def nothing(slot, tasks, *_):
                pass

            do = {"T1": T1, "T2": T2, "T3": T3, "TQK": TQK, "C": nothing, "S": S, "PT": PT, "PV": PV, "PT_P": PT_P,
                  "PO1": PO1, "PO2": PO2, "WS": nothing, "GM": nothing, "GT": GT, "EVQK": EVQK, "EVV": EVV,
                  "EVXP": EVXP, "EVGU": EVGU, "EVGV": EVGV, "EVOUT": EVOUT, "EVPJ": EVPJ,
                  "EVPL": EVPL, "N": N, "WF": WF, "F": F}

            def items(slot):
                for kind, *args in PLAN.get(slot, ()):
                    do[kind](slot, [aux.take() for _ in range(TASKS[kind])], *args)

            def run(first, end):
                for n in range(first, end):
                    if n + LEAD < GROUPS:
                        split_hi(n + LEAD)
                    if n == NG:
                        for _ in range(TB):
                            aux.take()
                    items(n)

            def HT(tasks, k, register=None):
                for a, task in enumerate(tasks):
                    bank = bank_full(task)
                    first = k + 2 * a if register is None else register * 4 + (k + 2 * a)
                    hi(bank, act_hi[:, bass.ds(first, 2)].rearrange("p k t -> p (k t)"))

            def hidden(n0, register):
                for j in range(2 * NG):
                    n = n0 + j
                    split_hi(n + LEAD)
                    if register is None:
                        items(n)
                    elif j == 2:
                        HT([aux.take(b) for b in HT_BANKS], 0, register)
                    if j == NG - 1:
                        act.wait_ge(s[f"pair_free{(C_FF + 1) % 2}"], c.value(f"pair_free{(C_FF + 1) % 2}"))
                        out_of(C_FF, n, [scratch[:, t] for t in range(TB)], ACT.Silu, 1)
                    if j == 2 * NG - 1:
                        ev(C_FF + 1)

            with act.Fori(0, DEPTH) as layer:
                c.layer, c.n = layer, {name: 0 for name in names}
                aux = Aux(c)
                act.wait_ge(s["layer_start"], layer + 1)
                for n in range(LEAD):
                    split_hi(n)
                items(-1)
                run(0, G_FF)
                hidden(G_FF, None)
                with act.Fori(0, N_FF - 1) as i:
                    c.enter(i, PER_FF)
                    hidden(G_FF + 2 * NG, i)
                c.leave(N_FF - 1)
                HT([aux.take(b) for b in HT_BANKS], 4 * (N_FF - 1))
                with act.Fori(0, N_DN // 2) as i:
                    c.enter(i, PER_DN)
                    for m in range(2 * NGD):
                        split_hi(G_DN + m + LEAD)
                        if m % NGD == NGD - 1:
                            ev(C_DN + m // NGD)
                c.leave(N_DN // 2)
                run(G_PJ, GROUPS)
                c.end_layer()

        @block.vector
        def _(dve):
            c = Counts(names)

            def split_lo(n):
                slot = n % RING
                dve.wait_ge(s["hi_ready"], c.value("hi_ready", n + 1))
                nc.vector.tensor_tensor(w_lo[:, slot], raw[:, slot], w_hi[:, slot].bitcast(F32), ALU.subtract
                                        ).then_inc(s["lo_ready"], 1)

            def bank_full(task):
                dve.wait_ge(s[f"aux_full{task[0]}"], task[2])
                return aux_ps[:, task[0]]

            def free(ins, task):
                ins.then_inc(s[f"aux_free{task[0]}"], 1)

            def chunk_done(slot):
                dve.wait_ge(s["mm_done"], c.value("mm_done", slot + 1))

            def step(ins):
                ins.then_inc(s["dve_step"], 1)
                c.add("dve_step")
                dve.wait_ge(s["dve_step"], c.value("dve_step"))

            def ask(ins):
                ins.then_inc(s["arg_ready"], 1)
                c.add("arg_ready")

            def answered(k=1):
                c.add("fn_ready", k)
                dve.wait_ge(s["fn_ready"], c.value("fn_ready"))

            def ev(chunk):
                c.add(f"pair_free{chunk % 2}")

            def pair_out(chunk):
                ev(chunk)
                dve.wait_ge(s[f"pair_free{chunk % 2}"], c.value(f"pair_free{chunk % 2}"))

            def lo(bank, dst_hi, dst, gain=None):
                if gain is None:
                    answered()
                    return nc.vector.tensor_tensor(dst, bank, dst_hi.bitcast(F32), ALU.subtract)
                return nc.vector.scalar_tensor_tensor(out=dst, in0=bank, scalar=gain, in1=dst_hi.bitcast(F32),
                                                      op0=ALU.mult, op1=ALU.subtract)

            def turned_h(tasks, col, dst_hi, dst, gain):
                for a, task in enumerate(tasks):
                    bank = bank_full(task)
                    answered(2)
                    for j in range(2):
                        k = 4 * col + 2 * a + j
                        ins = lo(bank[:, j * SEQ:(j + 1) * SEQ], dst_hi[:, k], dst[:, k],
                                 lg[:, gain + k:gain + k + 1])
                    free(ins, task)

            def N(slot, tasks, stage):
                answered()
                step(nc.vector.tensor_tensor(var, ssq[:, 0:4:2], ssq[:, 1:4:2], ALU.add))
                ask(nc.vector.tensor_scalar(var, var, 1.0 / D, EPS, ALU.mult, ALU.add))
                answered()
                ask(nc.vector.reciprocal(rstd[:, stage], dev))

            def norm_heads(x3, gain=None):
                sq = scratch[:].rearrange("p t (g c) -> p (t g) c", c=P)
                step(nc.vector.tensor_tensor(sq, x3, x3, ALU.mult))
                step(nc.vector.tensor_reduce(hss, sq, AX_X, ALU.add))
                ask(nc.vector.tensor_scalar(hvar, hss, 1.0 / HD, EPS, ALU.mult, ALU.add))
                answered()
                step(nc.vector.reciprocal(hr, hdev))
                ins = nc.vector.tensor_tensor(x3, x3, hr.unsqueeze(2).to_broadcast([P, TB * GRP, P]), ALU.mult)
                if gain is not None:
                    step(ins)
                    x = x3.rearrange("p (t g) c -> p t (g c)", t=TB)
                    ins = nc.vector.tensor_tensor(x, x, gain.unsqueeze(1).to_broadcast([P, TB, MIXW]), ALU.mult)
                ins.then_inc(s["norm_ready"], 1)
                c.add("norm_ready")

            def EVQK(slot, tasks, chunk, half, which):
                pair_out(chunk)
                norm_heads(qk_nat[:].rearrange("p t (g c) -> p (t g) c", c=P))

            def EVGV(slot, tasks, chunk):
                pair_out(chunk)
                norm_heads(gv[:].rearrange("p t g c -> p (t g) c"), v_gain[:])

            def TQK(slot, tasks, half, which):
                dst = (q_t, k_t)[which]
                for a, task in enumerate(tasks):
                    bank = bank_full(task)
                    free(nc.vector.tensor_scalar(dst[:, half, 2 * a:2 * a + 2].rearrange("p h t -> p (h t)"), bank,
                                                 lg[:, 48 + which:49 + which], (SCALE, 1.0)[which],
                                                 ALU.mult, ALU.mult), task)

            def WF(slot, tasks):
                answered()
                nc.vector.tensor_tensor(wf_lo[:], wf[:], wf_hi[:].bitcast(F32), ALU.subtract
                                        ).then_inc(s["wf_ready"], 1)

            def F(slot, tasks):
                for t, task in enumerate(forget):
                    bank = bank_full(task)
                    free(nc.vector.scalar_tensor_tensor(out=z[:, t], in0=bank[:, 0:HEADS], scalar=rstd[:, 0, t:t + 1],
                                                        in1=lf_bias[:], op0=ALU.mult, op1=ALU.add), task)
                for task in forget:
                    dve.wait_ge(s[f"aux_free{task[0]}"], task[3])
                step(nc.vector.tensor_scalar(nz, z, -1.0, None, ALU.mult))
                ask(nc.vector.tensor_tensor(nz, nz, z, ALU.min))
                step(nc.vector.tensor_scalar(logf, z, 0.0, None, ALU.min))
                answered()
                nc.vector.tensor_tensor(logf, logf, lnf, ALU.subtract).then_inc(s["gates_ready"], 1)
                c.add("gates_ready")

            def C(slot, tasks):
                bank = bank_full(tasks[0])
                step(nc.vector.tensor_copy(cum, bank[:, 0:TB * HEADS].rearrange("p (t h) -> p t h", t=TB)))
                free(nc.vector.tensor_scalar(neg_cum[:], bank[0:HEADS, P:P + SEQ], -1.0, None, ALU.mult), tasks[0])

            def S(slot, tasks, hd):
                bank = bank_full(tasks[0])
                pr = work[:, hd % 2].rearrange("p (t k) -> p t k", t=TB)
                for t, keys in ((0, P), (1, SEQ)):
                    ins = nc.vector.scalar_tensor_tensor(
                        out=pr[:, t, 0:keys], in0=bank[:, t * SEQ:t * SEQ + keys], scalar=cum[:, t, hd:hd + 1],
                        in1=mask[:, SEQ - keys:SEQ], op0=ALU.add, op1=ALU.add)
                free(ins, tasks[0])
                dve.wait_ge(s[f"aux_free{tasks[0][0]}"], tasks[0][3])
                nc.vector.tensor_reduce(mx[:, 0:1], pr[:, 0, 0:P], AX_X, ALU.max)
                step(nc.vector.tensor_reduce(mx[:, 1:2], pr[:, 1], AX_X, ALU.max))
                ask(nc.vector.tensor_scalar(nmx, mx, -1.0, None, ALU.mult))
                answered()
                step(nc.vector.reciprocal(rden, den))
                for t, keys in ((0, P), (1, SEQ)):
                    ins = nc.vector.tensor_scalar(pr[:, t, 0:keys], pr[:, t, 0:keys], rden[:, t:t + 1], None, ALU.mult)
                ins.then_inc(s["probs_ready"], 1)
                c.add("probs_ready")

            def PV(slot, tasks, hd):
                bank = bank_full(tasks[0])
                free(lo(bank[:, 0:SEQ], act_hi[:, KT + hd], act_lo[:, KT + hd]), tasks[0])

            def PT_P(slot, tasks):
                bank = bank_full(tasks[0])
                free(lo(bank, pt_hi[:].rearrange("p k t -> p (k t)"), pt_lo[:].rearrange("p k t -> p (k t)")), tasks[0])

            def PO2(slot, tasks, g):
                bank = bank_full(tasks[0])
                k = KT + HEADS + GRP + g
                answered()
                free(lo(bank[:, 0:SEQ], act_hi[:, k], act_lo[:, k], lg[:, 50 + g:51 + g]), tasks[0])

            def WS(slot, tasks):
                bank = bank_full(tasks[0])
                free(nc.vector.tensor_tensor(w_st[:], bank.rearrange("p (g t) -> p g t", g=GRP),
                                             upper.unsqueeze(1).to_broadcast([P, GRP, P]), ALU.mult), tasks[0])

            def GM(slot, tasks):
                for t, task in enumerate(tasks):
                    bank = bank_full(task)
                    for g in range(GRP):
                        ins = nc.vector.scalar_tensor_tensor(
                            out=gu[:, t, g], in0=bank[:, g * P:(g + 1) * P], scalar=lg[:, 54 + g:55 + g],
                            in1=gu[:, t, g], op0=ALU.add, op1=ALU.mult)
                    free(ins, task)

            def GT(slot, tasks):
                for a, task in enumerate(tasks):
                    bank = bank_full(task)
                    k = KT + HEADS + 2 * a
                    free(lo(bank, act_hi[:, k:k + 2].rearrange("p k t -> p (k t)"),
                            act_lo[:, k:k + 2].rearrange("p k t -> p (k t)")), task)

            def T1(slot, tasks, col):
                turned_h(tasks, col, act_hi, act_lo, 0)

            def T2(slot, tasks, col):
                turned_h(tasks, col, xn_hi, xn_lo, KT)

            def T3(slot, tasks, col):
                turned_h(tasks, col, xn_hi, xn_lo, 2 * KT)

            def add_to_h(chunk, n, cols):
                chunk_done(n)
                nc.vector.tensor_tensor(h[:, :, cols], h[:, :, cols], acc[:, chunk % 2], ALU.add
                                        ).then_inc(s[f"pair_free{chunk % 2}"], 1)
                ev(chunk)

            def EVOUT(slot, tasks, chunk, col):
                add_to_h(chunk, slot, slice(col * COLS, (col + 1) * COLS))

            def EVPL(slot, tasks, chunk, col):
                pair_out(chunk)
                cols = slice(col * COLS, (col + 1) * COLS)
                step(nc.vector.tensor_tensor(work[:], scratch[:], ple[:, col], ALU.mult))
                nc.vector.tensor_tensor(h[:, :, cols], h[:, :, cols], work[:], ALU.add).then_inc(s["h_ready"], 1)
                c.add("h_ready")

            def counted(slot, tasks, chunk, *_):
                ev(chunk)

            def nothing(slot, tasks, *_):
                pass

            do = {"T1": T1, "T2": T2, "T3": T3, "TQK": TQK, "C": C, "S": S, "PT": nothing, "PV": PV, "PT_P": PT_P,
                  "PO1": nothing, "PO2": PO2, "WS": WS, "GM": GM, "GT": GT, "EVQK": EVQK, "EVV": counted,
                  "EVXP": counted, "EVGU": counted, "EVGV": EVGV, "EVOUT": EVOUT, "EVPJ": counted,
                  "EVPL": EVPL, "N": N, "WF": WF, "F": F}

            def items(slot):
                for kind, *args in PLAN.get(slot, ()):
                    do[kind](slot, [aux.take() for _ in range(TASKS[kind])], *args)

            forget = []

            def run(first, end):
                for n in range(first, end):
                    if n + LEAD < GROUPS:
                        split_lo(n + LEAD)
                    if n == NG:
                        forget[:] = [aux.take() for _ in range(TB)]
                    items(n)

            def HT(tasks, k, register=None):
                for a, task in enumerate(tasks):
                    bank = bank_full(task)
                    first = k + 2 * a if register is None else register * 4 + (k + 2 * a)
                    free(lo(bank, act_hi[:, bass.ds(first, 2)].rearrange("p k t -> p (k t)"),
                            act_lo[:, bass.ds(first, 2)].rearrange("p k t -> p (k t)")), task)

            def hidden(n0, register):
                for j in range(2 * NG):
                    n = n0 + j
                    split_lo(n + LEAD)
                    if register is None:
                        items(n)
                    elif j == 2:
                        HT([aux.take(b) for b in HT_BANKS], 0, register)
                    if j == NG - 1:
                        ev(C_FF)
                    if j == 2 * NG - 1:
                        gate = f"pair_free{C_FF % 2}"
                        dve.wait_ge(s[gate], c.value(gate))
                        chunk_done(n)
                        for t in range(TB):
                            ins = nc.vector.scalar_tensor_tensor(
                                out=work[:, t], in0=acc[:, (C_FF + 1) % 2, t], scalar=rstd[:, 1, t:t + 1],
                                in1=scratch[:, t], op0=ALU.mult, op1=ALU.mult)
                        ins.then_inc(s[f"pair_free{(C_FF + 1) % 2}"], 1)
                        ev(C_FF + 1)

            dve.wait_ge(gains_t, 1)
            nc.vector.tensor_copy(gains[:], aux_ps[:, 0, 0:2 * 58]).then_inc(gains_in, 1)
            dve.wait_ge(gains_in, 1)
            dve.wait_ge(x_in, 16)
            with dve.Fori(0, DEPTH) as layer:
                c.layer, c.n = layer, {name: 0 for name in names}
                aux = Aux(c)
                nc.vector.tensor_copy(lf_bias[:], f_bias[:, bass.ds(layer * HEADS, HEADS)])
                nc.vector.tensor_copy(lg[:], gains[:, bass.ds(layer * 58, 58)]).then_inc(s["layer_start"], 1)
                dve.wait_ge(s["layer_start"], layer + 1)
                for n in range(LEAD):
                    split_lo(n)
                items(-1)
                run(0, G_FF)
                hidden(G_FF, None)
                with dve.Fori(0, N_FF - 1) as i:
                    c.enter(i, PER_FF)
                    hidden(G_FF + 2 * NG, i)
                c.leave(N_FF - 1)
                HT([aux.take(b) for b in HT_BANKS], 4 * (N_FF - 1))
                with dve.Fori(0, N_DN // 2) as i:
                    c.enter(i, PER_DN)
                    for m in range(2 * NGD):
                        split_lo(G_DN + m + LEAD)
                        if m % NGD == NGD - 1:
                            add_to_h(C_DN + m // NGD, G_DN + m, bass.ds(i * (2 * COLS) + m // NGD * COLS, COLS))
                c.leave(N_DN // 2)
                run(G_PJ, GROUPS)
                c.end_layer()


_INS = ["x", "p", "norm_mix", "w_in", "q_norm", "k_norm", "forget_bias", "gmlp_v_norm", "gmlp_w_s", "gmlp_b_s",
        "pool_w", "pool_scale", "w_out", "norm_ffn", "w_ffn_gate", "w_ffn_up", "w_ffn_down", "norm_ple",
        "w_ple_gate", "w_ple_proj"]


def shape_constants():
    i = np.arange(P)
    upper = (i[:, None] <= i[None, :]).astype(np.float32)
    mask = np.where(i[None, :] <= i[:, None], 0.0, MASKED).astype(np.float32)
    consts = np.concatenate([np.eye(P, dtype=np.float32), upper, np.ones((P, P), np.float32),
                             np.zeros((P, P), np.float32), mask], axis=1)
    t = np.arange(SEQ)
    bands = np.zeros((P, GRP, 3, P), np.float32)
    for g, win in enumerate(WINDOWS):
        count = np.minimum(t + 1, win).astype(np.float32)
        inside = (t[:, None] <= t[None, :]) & (t[:, None] > t[None, :] - win)
        full = (inside / count[None, :] - np.eye(SEQ)).astype(np.float32)
        bands[:, g, 0], bands[:, g, 1], bands[:, g, 2] = full[:P, :P], full[:P, P:], full[P:, P:]
    return consts, bands


def kernel(**inputs):
    import concourse.bacc as _bacc
    from concourse.bass_utils import run_bass_kernel_spmd as _run

    nc = _bacc.Bacc("TRN2", target_bir_lowering=False, num_devices=1)
    consts, bands = shape_constants()
    arrays, args = {}, []
    for name, a in [(n, inputs[n]) for n in _INS] + [("consts", consts), ("bands", bands)]:
        a = np.ascontiguousarray(a)
        arrays[f"in_{name}_dram"] = a
        args.append(nc.dram_tensor(f"in_{name}_dram", a.shape, mybir.dt.from_np(a.dtype), kind="ExternalInput").ap())
    args.append(nc.dram_tensor("out_0_dram", (1, SEQ, D), F32, kind="ExternalOutput").ap())
    trunk(nc, *args)
    r = _run(nc, [arrays], core_ids=[0])
    return r.results[0]["out_0_dram"]
```

```python
from contextlib import ExitStack

import numpy as np

import concourse.bass as bass
from concourse import mybir

F32 = mybir.dt.float32
F32R = mybir.dt.float32r
ALU = mybir.AluOpType
ACT = mybir.ActivationFunctionType
AX_X = mybir.AxisListType.X

P = 128
COLS = 512
GK = 2
RING = 4
LEAD = 3
SEQ = 256
TB = SEQ // P
D = 2048
KT = D // P
D_FF = 5632
FKT = D_FF // P
HD = 128
HEADS = 8
HALF = HEADS // 2
ATTN = HEADS * HD
GRP = 4
MIXW = GRP * P
D_PLE = 256
DEPTH = 2
EPS = 1e-6
SCALE = float(HD) ** -0.5
MASKED = -1e38
LO_ROW = 32
WINDOWS = (2, 4, 8, 16)

F_COL = 3 * ATTN
GU_COL = F_COL + HEADS
GV_COL = GU_COL + MIXW
XP_COL = GV_COL + MIXW
IN_COLS = [0, ATTN, 2 * ATTN, COLS, ATTN + COLS, 2 * ATTN + COLS, GV_COL, GU_COL, XP_COL]
NG = KT // GK
NGD = FKT // GK
N_IN, N_OUT, N_FF, N_DN, N_PJ, N_PL = 9, D // COLS, D_FF // COLS, D // COLS, D // COLS, D // COLS
G_OUT = N_IN * NG
G_FF = G_OUT + N_OUT * NG
G_DN = G_FF + 2 * N_FF * NG
G_PJ = G_DN + N_DN * NGD
G_PL = G_PJ + N_PJ
GROUPS = G_PL + N_PL * NG
C_OUT = N_IN
C_FF = C_OUT + N_OUT
C_DN = C_FF + 2 * N_FF
C_PJ = C_DN + N_DN
C_PL = C_PJ + N_PJ
CHUNKS = C_PL + N_PL

TASKS = {"T1": 2, "T2": 2, "T3": 2, "EVQK": 0, "EVV": 0, "EVXP": 0, "EVGU": 0, "EVGV": 0, "TQK": 2,
         "WF": 0, "FM": 1, "FT": 1, "F": 0, "C": 1, "S": 1, "PT": 1, "PV": 1, "PT_P": 1, "PO1": 1, "PO2": 1, "WS": 1,
         "NRM": 0, "SX": 0, "FX": 0, "GM": 2, "GT": 2, "EVOUT": 0, "N": 0,
         "EVPJ": 0, "EVPL": 0}


def make_plan():
    plan = {}

    def put(slot, kind, *args):
        plan.setdefault(slot, []).append((kind, *args))

    for c, slot in enumerate((-1, 0, 1, 3)):
        put(slot, "T1", c)
    put(4, "N", 0)
    put(6, "WF")
    for half in range(2):
        c0 = 3 * half
        put(NG * c0 + NG - 1, "EVQK", c0, half, 0)
        put(NG * c0 + NG, "NRM")
        put(NG * c0 + NG + 2, "TQK", half, 0)
        put(NG * (c0 + 1) + NG - 1, "EVQK", c0 + 1, half, 1)
        put(NG * (c0 + 1) + NG, "NRM")
        put(NG * (c0 + 1) + NG + 2, "TQK", half, 1)
        put(NG * (c0 + 2) + NG - 1, "EVV", c0 + 2, half)
    put(NG, "FM")
    put(NG + 4, "FT")
    put(2 * NG + 1, "F")
    put(2 * NG + 3, "FX")
    put(2 * NG + 5, "C")
    put(2 * NG + 6, "PT_P")
    for h in range(HEADS):
        put(3 * NG + 6 * h, "S", h)
        put(3 * NG + 6 * h + 1, "SX", h)
        put(3 * NG + 6 * h + 3, "PT", h)
        put(3 * NG + 6 * h + 5, "PV", h)
    put(7 * NG - 1, "EVGV", 6)
    put(7 * NG, "NRM", True)
    put(7 * NG + 2, "WS")
    put(8 * NG - 1, "EVGU", 7)
    put(8 * NG + 1, "GM")
    put(8 * NG + 3, "GT")
    put(9 * NG - 1, "EVXP", 8)
    for g in range(GRP):
        put(G_OUT + 1 + g // 2, "PO1", g)
        put(G_OUT + 3 + g // 2, "PO2", g)
    for c in range(N_OUT):
        put(G_OUT + NG * c + NG - 1, "EVOUT", C_OUT + c, c)
        put(G_OUT + NG * (c + 1) + 1, "T2", c)
    put(G_FF + 3, "N", 1)
    put(G_PJ, "T3", 0)
    put(G_PJ, "T3", 1)
    put(G_PJ + 1, "T3", 2)
    put(G_PJ + 2, "T3", 3)
    for c in range(N_PJ):
        put(G_PJ + c, "EVPJ", C_PJ + c, c)
    put(G_PL + 2, "N", 2)
    for c in range(N_PL):
        put(G_PL + NG * c + NG - 1, "EVPL", C_PL + c, c)
    return plan


PLAN = make_plan()

AUX = 4
HT_BANKS = (0, 1)


def aux_uses():
    n = sum(TASKS[kind] for items in PLAN.values() for kind, *_ in items)
    uses = [len(range(b, n, AUX)) for b in range(AUX)]
    for b in HT_BANKS:
        uses[b] += N_FF
    return uses


PER_LAYER = {"mm_done": GROUPS, "hi_ready": GROUPS, "lo_ready": GROUPS,
             "pair_free0": (CHUNKS + 1) // 2, "pair_free1": CHUNKS // 2,
             "norm_ready": 5, "gates_ready": 1, "probs_ready": HEADS, "h_ready": N_PL,
             "small_in": 5 * 16, "wf_in": 16, "layer_start": 1, "wf_ready": 1, "raw": GROUPS // RING,
             "fn_ready": 107, "arg_ready": 20, "act_step": 10, "dve_step": 43}
for _b, _n in enumerate(aux_uses()):
    PER_LAYER[f"aux_full{_b}"] = PER_LAYER[f"aux_free{_b}"] = _n
PER_FF = {"mm_done": 2 * NG, "hi_ready": 2 * NG, "lo_ready": 2 * NG, "pair_free0": 1, "pair_free1": 1,
          "aux_full0": 1, "aux_full1": 1, "aux_free0": 1, "aux_free1": 1,
          "raw": 2 * NG // RING, "fn_ready": 2}
PER_DN = {"mm_done": 2 * NGD, "hi_ready": 2 * NGD, "lo_ready": 2 * NGD, "pair_free0": 1, "pair_free1": 1,
          "raw": 2 * NGD // RING}
CREDIT = {"h_ready": N_PL, "lo_ready": RING, "mm_done": RING, "pair_free0": 1, "pair_free1": 1,
          **{f"aux_free{b}": 1 for b in range(AUX)}}


class Counts:

    def __init__(self, names):
        self.n = {name: 0 for name in names}
        self.layer = 0
        self.loop = None

    def value(self, name, n=None):
        n = self.n[name] if n is None else n
        v = self.layer * PER_LAYER[name] + (CREDIT.get(name, 0) + n)
        if self.loop is not None:
            v = v + self.loop[0] * self.loop[1].get(name, 0)
        return v

    def add(self, name, k=1):
        self.n[name] += k

    def enter(self, register, step):
        self.loop, self.before = (register, step), dict(self.n)

    def leave(self, passes):
        for name, n in self.n.items():
            step = self.loop[1].get(name, 0)
            assert n - self.before[name] in (0, step), (name, n - self.before[name], step)
            if n != self.before[name]:
                self.n[name] = self.before[name] + passes * step
        self.loop = None

    def end_layer(self):
        off = {k: (n, PER_LAYER[k]) for k, n in self.n.items() if n and n != PER_LAYER[k]}
        assert not off, off


class Aux:

    def __init__(self, counts):
        self.counts, self.turn = counts, 0

    def take(self, bank=None):
        if bank is None:
            bank, self.turn = self.turn % AUX, self.turn + 1
        full, free = f"aux_full{bank}", f"aux_free{bank}"
        before = self.counts.value(free)
        self.counts.add(full)
        self.counts.add(free)
        return bank, before, self.counts.value(full), self.counts.value(free)


def trunk(nc, x, p, norm_mix, w_in, q_norm, k_norm, forget_bias, gmlp_v_norm, gmlp_w_s, gmlp_b_s, pool_w,
          pool_scale, w_out, norm_ffn, w_ffn_gate, w_ffn_up, w_ffn_down, norm_ple, w_ple_gate, w_ple_proj,
          consts, bands, out):
    with ExitStack() as ctx:
        def sb(name, shape, dt=F32):
            return ctx.enter_context(nc.sbuf_tensor(name, shape, dt))

        def sem(name):
            return ctx.enter_context(nc.semaphore(name))

        h = sb("h", [P, TB, D])
        raw = sb("raw", [P, RING, GK, COLS])
        w_hi = sb("w_hi", [P, RING, GK, COLS], F32R)
        w_lo = sb("w_lo", [P, RING, GK, COLS], F32R)
        BYTES = {"act_hi": FKT * SEQ * 4, "act_lo": FKT * SEQ * 4, "xn_hi": KT * SEQ * 4, "xn_lo": KT * SEQ * 4}
        OFFSET, at = {}, (nc.sbuf_base + 31) // 32 * 32
        sb("arena", [P, sum(BYTES.values()) // 4])
        for name, size in BYTES.items():
            OFFSET[name], at = at, at + size
        act_hi, act_lo, xn_hi, xn_lo = (nc.alloc_sbuf_tensor_at(
            name, [P, BYTES[name] // 4 // SEQ, SEQ], F32R, offset=OFFSET[name]) for name in BYTES)
        pt_hi = sb("pt_hi", [P, 2, SEQ], F32R)
        pt_lo = sb("pt_lo", [P, 2, SEQ], F32R)
        scratch = sb("scratch", [P, TB, COLS])
        work = sb("work", [P, TB, COLS])
        p_nat = sb("p_nat", [P, TB, D_PLE])
        const = sb("const", [P, 5 * P + HEADS])
        gain_rows = scratch[:].rearrange("p t n -> p (t n)")[0:2 * 58, 0:P]
        gains = sb("gains", [P, 2 * 58])
        lg = sb("lg", [P, 58])
        f_bias = sb("f_bias", [P, DEPTH * HEADS])
        lf_bias = sb("lf_bias", [P, HEADS])
        f_rows = work[0:2 * HEADS, 0, 0:SEQ]
        wf = sb("wf", [P, KT, HEADS])
        wf_hl = sb("wf_hl", [P, KT, 2 * HEADS], F32R)
        wf_hi, wf_lo = wf_hl[:, :, 0:HEADS], wf_hl[:, :, HEADS:2 * HEADS]
        w_st = sb("w_st", [P, GRP, P])
        stat = sb("stat", [P, 128])

        ident = const[:, 0:P]
        upper = const[:, P:2 * P]
        ones = const[:, 2 * P:3 * P]
        both_rows = const[0:LO_ROW + HEADS, 5 * P:5 * P + HEADS]
        mask = const[:, 3 * P:5 * P]

        def over(name, host, first, shape):
            assert first + int(np.prod(shape[1:])) * 4 <= BYTES[host]
            return nc.alloc_sbuf_tensor_at(name, shape, F32, offset=OFFSET[host] + first)

        K = 1024
        v_nat = over("v_nat", "xn_hi", 0, [P, 2, TB, COLS])
        qk_nat = over("qk_nat", "xn_hi", 8 * K, [P, TB, COLS])
        probs_t = over("probs_t", "xn_hi", 12 * K, [P, 2, 3 * P])
        pool_d = over("pool_d", "xn_lo", 8 * K, [P, GRP, SEQ])
        q_t = over("q_t", "xn_lo", 0, [P, 2, HALF, SEQ])
        k_t = over("k_t", "xn_lo", 8 * K, [P, 2, HALF, SEQ])
        tail = 2 * KT * SEQ * 4
        gu = over("gu", "act_hi", tail, [P, TB, GRP, P])
        gv = over("gv", "act_hi", tail + 4 * K, [P, TB, GRP, P])
        xp = over("xp", "act_hi", tail + 8 * K, [P, TB, COLS])
        v_gain = over("v_gain", "act_lo", tail, [P, MIXW])
        w_s = over("w_s", "act_lo", tail + 2 * K, [P, GRP, P])
        w_pool = over("w_pool", "act_lo", tail + 4 * K, [P, GRP, P])
        band = over("band", "act_lo", tail + 6 * K, [P, GRP, 3, P])
        ple = over("ple", "act_lo", KT * SEQ * 4, [P, N_PJ, TB, COLS])

        ssq, var, rstd = stat[:, 0:4], stat[:, 4:6], stat[:, 6:12].rearrange("p (s t) -> p s t", s=3)
        dev = stat[:, 12:14]
        hss, hvar, hdev, hr = (stat[:, a:a + 8] for a in (16, 24, 32, 40))
        fstat = sb("fstat", [P, 7, TB, HEADS])
        z, nz, ef, lnf, logf, cum, fsum = (fstat[:, a] for a in range(7))
        neg_cum = sb("neg_cum", [LO_ROW + HEADS, SEQ], F32R)
        both = sb("both", [LO_ROW + HEADS, HEADS], F32R)
        mx, nmx, den, rden = (stat[:, a:a + 2] for a in (48, 50, 52, 54))

        acc = ctx.enter_context(nc.psum_tensor("acc", [P, 2, TB, COLS], F32))
        aux_ps = ctx.enter_context(nc.psum_tensor("aux_ps", [P, AUX, COLS], F32))

        raw_in = [sem(f"raw_in{i}") for i in range(RING)]
        x_in = [sem(f"x_in{i}") for i in range(N_PL)]
        start_in, out_sent = sem("start_in"), sem("out_sent")
        s = {name: sem(name) for name in PER_LAYER if name != "raw"}
        gains_t, gains_in = sem("gains_t"), sem("gains_in")
        names = list(PER_LAYER)

        h_of = lambda t: t.rearrange("b (t p) n -> p (b t) n", p=P)

        def group_of(w, layer, k, col, width=COLS):
            return w[bass.ds(layer, 1), bass.ds(k * (GK * P), GK * P), bass.ds(col, width)].rearrange(
                "l (j p) n -> p (l j) n", p=P)

        block = ctx.enter_context(nc.Block())

        @block.sync
        def _(sp):
            sp.sem_inc(s["lo_ready"], RING)
            c = Counts(names)

            def load(n, src):
                slot = n % RING
                sp.wait_ge(s["lo_ready"], c.value("lo_ready", n - RING + 1))
                sp.dma_start(raw[:, slot], src).then_inc(raw_in[slot], 16)

            sp.dma_start(h[:, :, 0:COLS], h_of(x)[:, :, 0:COLS]).then_inc(x_in[0], 16)
            with sp.Fori(0, DEPTH) as layer:
                c.layer = layer
                for i, col in enumerate(IN_COLS):
                    for k in range(NG):
                        load(i * NG + k, group_of(w_in, layer, k, col))
                        if i == k == 0:
                            sp.wait_ge(start_in, 9 * 16)
                with sp.Fori(0, N_OUT) as i:
                    c.loop = (i, {"lo_ready": NG})
                    for k in range(NG):
                        load(G_OUT + k, group_of(w_out, layer, k, i * COLS))
                with sp.Fori(0, N_FF) as i:
                    c.loop = (i, PER_FF)
                    for half, w in enumerate((w_ffn_gate, w_ffn_up)):
                        for k in range(NG):
                            load(G_FF + half * NG + k, group_of(w, layer, k, i * COLS))
                with sp.Fori(0, N_DN // 2) as i:
                    c.loop = (i, PER_DN)
                    for m in range(2 * NGD):
                        load(G_DN + m, group_of(w_ffn_down, layer, m % NGD, i * (2 * COLS) + m // NGD * COLS))
                c.loop = None
                for i in range(N_PJ):
                    load(G_PJ + i, group_of(w_ple_proj, layer, 0, i * COLS))
                with sp.Fori(0, N_PL) as i:
                    c.loop = (i, {"lo_ready": NG})
                    for k in range(NG):
                        load(G_PL + k, group_of(w_ple_gate, layer, k, i * COLS))
                c.loop = None
            for i in range(N_PL):
                cols = slice(i * COLS, (i + 1) * COLS)
                sp.wait_ge(s["h_ready"], CREDIT["h_ready"] + (DEPTH - 1) * N_PL + i + 1)
                sp.dma_start(h_of(out)[:, :, cols], h[:, :, cols]).then_inc(out_sent, 16)
            sp.wait_ge(out_sent, 16 * N_PL)

        @block.gpsimd
        def _(pool):
            with pool.Fori(0, DEPTH) as layer:
                pool.wait_ge(s["mm_done"], layer * GROUPS + RING + 2)
                pool.dma_start(wf[:], w_in[bass.ds(layer, 1), :, F_COL:F_COL + HEADS].rearrange(
                    "l (k p) n -> p (l k) n", p=P)).then_inc(s["wf_in"], 16)
                for dst, src in (
                    (p_nat[:], p[bass.ds(layer, 1)].rearrange("l b (t p) n -> p (l b t) n", p=P)),
                    (v_gain[:], gmlp_v_norm[bass.ds(layer, 1)].rearrange("l g c -> (l g c)").partition_broadcast(P)),
                    (w_s[:], gmlp_w_s[bass.ds(layer, 1)].rearrange("l g t s -> t (l g) s")),
                    (w_pool[:], pool_w[bass.ds(layer, 1)].rearrange("l g c d -> c (l g) d")),
                    (band[:], bands),
                ):
                    pool.dma_start(dst, src).then_inc(s["small_in"], 16)

        @block.tensor
        def _(pe):
            c = Counts(names)
            for name in ("pair_free0", "pair_free1", *(f"aux_free{b}" for b in range(AUX))):
                pe.sem_inc(s[name], 1)
            done = {}

            def claim(task, *needs):
                evacuated(*(t for t in needs if t[0] != task[0]))
                pe.wait_ge(s[f"aux_free{task[0]}"], task[1])
                return aux_ps[:, task[0]]

            def evacuated(*tasks):
                for bank, value in {t[0]: t[3] for t in tasks}.items():
                    pe.wait_ge(s[f"aux_free{bank}"], value)

            def filled(ins, task):
                ins.then_inc(s[f"aux_full{task[0]}"], 1)

            def group(n, tiles, hi, lo, chunk, first, last):
                slot = n % RING
                c.add("lo_ready")
                c.add("mm_done")
                pe.wait_ge(s["lo_ready"], c.value("lo_ready"))
                if first:
                    pe.wait_ge(s[f"pair_free{chunk % 2}"], c.value(f"pair_free{chunk % 2}"))
                for j, k in enumerate(tiles):
                    for t in range(TB):
                        ps = acc[:, chunk % 2, t, :]
                        x_hi, x_lo = (a[:, k, t * P:(t + 1) * P] for a in (hi, lo))
                        a = first and j == 0
                        z_ = last and j == len(tiles) - 1
                        pe.matmul(ps, x_hi, w_hi[:, slot, j, :], start=a, stop=False)
                        pe.matmul(ps, x_hi, w_lo[:, slot, j, :], start=False, stop=False)
                        mm = pe.matmul(ps, x_lo, w_hi[:, slot, j, :], start=False, stop=z_)
                mm.then_inc(s["mm_done"], 1)

            def turn(task, blocks, *needs):
                bank = claim(task, *needs)
                for i, b in enumerate(blocks):
                    t = pe.transpose(bank[:, i * P:(i + 1) * P], b, ident)
                filled(t, task)

            def turn_h(tasks, col):
                for a, task in enumerate(tasks):
                    turn(task, [h[:, t, (4 * col + 2 * a + j) * P:(4 * col + 2 * a + j + 1) * P]
                                for j in range(2) for t in range(TB)])

            def T1(tasks, col):
                pe.wait_ge(x_in[col], 16)
                pe.wait_ge(s["h_ready"], c.value("h_ready", col + 1 - N_PL))
                turn_h(tasks, col)

            def T2(tasks, col):
                pair = f"pair_free{(C_OUT + col) % 2}"
                pe.wait_ge(s[pair], done[("h", C_OUT + col)])
                turn_h(tasks, col)

            def T3(tasks, col):
                if col == 0:
                    for pair in ("pair_free0", "pair_free1"):
                        pe.wait_ge(s[pair], done[("down", pair)])
                turn_h(tasks, col)

            def TQK(tasks, half, which):
                c.add("norm_ready")
                pe.wait_ge(s["norm_ready"], c.value("norm_ready"))
                for a, task in enumerate(tasks):
                    turn(task, [qk_nat[:, t, (2 * a + j) * P:(2 * a + j + 1) * P]
                                for j in range(2) for t in range(TB)])
                done[("qk", half, which)] = tasks

            def FM(tasks):
                (task,) = tasks
                pe.wait_ge(s["wf_ready"], c.value("wf_ready", 1))
                bank = claim(task)
                for k in range(KT):
                    pe.matmul(bank[0:2 * HEADS, 0:SEQ], wf_hl[:, k], act_hi[:, k], start=k == 0, stop=False)
                    mm = pe.matmul(bank[0:HEADS, 0:SEQ], wf_hi[:, k], act_lo[:, k], start=False, stop=k == KT - 1)
                filled(mm, task)
                done["fm"] = task

            def FT(tasks):
                (task,) = tasks
                bank = claim(task, done["fm"])
                for t in range(TB):
                    mm = pe.matmul(bank[:, t * 2 * HEADS:(t + 1) * 2 * HEADS], f_rows[:, t * P:(t + 1) * P],
                                   ident[0:2 * HEADS, 0:2 * HEADS], start=True, stop=True)
                filled(mm, task)

            def C(tasks):
                (task,) = tasks
                bank = claim(task)
                c.add("gates_ready")
                pe.wait_ge(s["gates_ready"], c.value("gates_ready"))
                pe.matmul(bank[:, 0:HEADS], upper, logf[:, 0], start=True, stop=True)
                pe.matmul(bank[:, HEADS:2 * HEADS], ones, logf[:, 0], start=True, stop=False)
                pe.matmul(bank[:, HEADS:2 * HEADS], upper, logf[:, 1], start=False, stop=True)
                row = bank[0:HEADS, P:P + SEQ]
                pe.matmul(row[:, 0:P], logf[:, 0], upper, start=True, stop=True)
                pe.matmul(row[:, P:SEQ], logf[:, 0], ones, start=True, stop=False)
                filled(pe.matmul(row[:, P:SEQ], logf[:, 1], upper, start=False, stop=True), task)
                done["c"] = task

            def S(tasks, hd):
                (task,) = tasks
                half, i = divmod(hd, HALF)
                needs = () if i else (*done[("qk", half, 0)], *done[("qk", half, 1)], *(() if half else (done["c"],)))
                bank = claim(task, *needs)
                for t, keys in ((0, P), (1, SEQ)):
                    o = bank[:, t * SEQ:t * SEQ + keys]
                    pe.matmul(o, q_t[:, half, i, t * P:(t + 1) * P], k_t[:, half, i, 0:keys], start=True, stop=False)
                    mm = pe.matmul(o, both[:, hd:hd + 1].to_broadcast([LO_ROW + HEADS, P]),
                                   neg_cum[:, 0:keys], start=False, stop=True)
                filled(mm, task)

            def PT(tasks, hd):
                c.add("probs_ready")
                pe.wait_ge(s["probs_ready"], c.value("probs_ready"))
                pr = work[:, hd % 2].rearrange("p (t k) -> p t k", t=TB)
                turn(tasks[0], [pr[:, 0, 0:P], pr[:, 1, 0:P], pr[:, 1, P:SEQ]])
                done[("pt", hd)] = tasks[0]

            def PV(tasks, hd):
                (task,) = tasks
                half, i = divmod(hd, HALF)
                if i == 0:
                    pe.wait_ge(s[f"pair_free{(3 * half + 2) % 2}"], done[("v", half)])
                bank = claim(task, done[("pt", hd)])
                cols = slice(i * HD, (i + 1) * HD)
                pt = probs_t[:, hd % 2]
                pe.matmul(bank[:, 0:SEQ], v_nat[:, half, 0, cols], pt[:, 0:SEQ], start=True, stop=False)
                filled(pe.matmul(bank[:, P:SEQ], v_nat[:, half, 1, cols], pt[:, SEQ:3 * P],
                                 start=False, stop=True), task)

            def PT_P(tasks):
                pe.wait_ge(s["small_in"], c.value("small_in", PER_LAYER["small_in"]))
                turn(tasks[0], [p_nat[:, t, j * P:(j + 1) * P] for j in range(2) for t in range(TB)])
                done["p"] = tasks[0]

            def PO1(tasks, g):
                (task,) = tasks
                if g == 0:
                    pe.wait_ge(s["pair_free0"], done["xp"])
                bank = claim(task)
                cols = slice(g * P, (g + 1) * P)
                pe.matmul(bank[:, 0:SEQ], xp[:, 0, cols], band[:, g, 0:2].rearrange("p a b -> p (a b)"),
                          start=True, stop=False)
                filled(pe.matmul(bank[:, P:SEQ], xp[:, 1, cols], band[:, g, 2], start=False, stop=True), task)
                done[("po", g)] = task

            def PO2(tasks, g):
                bank = claim(tasks[0], done[("po", g)])
                filled(pe.matmul(bank[:, 0:SEQ], w_pool[:, g], pool_d[:, g], start=True, stop=True), tasks[0])

            def WS(tasks):
                turn(tasks[0], [w_s[:, g] for g in range(GRP)])
                done["ws"] = tasks[0]

            def GM(tasks):
                c.add("norm_ready")
                pe.wait_ge(s["norm_ready"], c.value("norm_ready"))
                for t, task in enumerate(tasks):
                    bank = claim(task, done["ws"])
                    for g in range(GRP):
                        mm = pe.matmul(bank[:, g * P:(g + 1) * P], w_st[:, g], gv[:, t, g], start=True, stop=True)
                    filled(mm, task)
                done["gm"] = tasks

            def GT(tasks):
                for a, task in enumerate(tasks):
                    turn(task, [gu[:, t, 2 * a + j] for j in range(2) for t in range(TB)], *done["gm"])
                done["gt"] = tasks

            def HT(tasks):
                pe.wait_ge(s[f"pair_free{(C_FF + 1) % 2}"], c.value(f"pair_free{(C_FF + 1) % 2}"))
                for a, task in enumerate(tasks):
                    turn(task, [work[:, t, (2 * a + j) * P:(2 * a + j + 1) * P]
                                for j in range(2) for t in range(TB)])

            def ev(chunk):
                c.add(f"pair_free{chunk % 2}")
                return c.value(f"pair_free{chunk % 2}")

            def EVV(tasks, chunk, half):
                done[("v", half)] = ev(chunk)

            def EVXP(tasks, chunk):
                done["xp"] = ev(chunk)

            def EVOUT(tasks, chunk, col):
                done[("h", chunk)] = ev(chunk)

            def counted(tasks, chunk, *_):
                ev(chunk)

            def nothing(tasks, *_):
                pass

            do = {"T1": T1, "T2": T2, "T3": T3, "TQK": TQK, "FM": FM, "FT": FT, "C": C, "S": S,
                  "PT": PT, "PV": PV, "PT_P": PT_P,
                  "PO1": PO1, "PO2": PO2, "WS": WS, "GM": GM, "GT": GT, "EVQK": counted, "EVV": EVV,
                  "EVXP": EVXP, "EVGU": counted, "EVGV": counted, "EVOUT": EVOUT, "EVPJ": counted,
                  "EVPL": counted, "N": nothing, "WF": nothing, "F": nothing,
                  "NRM": nothing, "SX": nothing, "FX": nothing}

            def items(slot):
                for kind, *args in PLAN.get(slot, ()):
                    tasks = [aux.take() for _ in range(TASKS[kind])]
                    do[kind](tasks, *args)
                    if kind in ("T1", "T2", "T3"):
                        done[(kind, args[0])] = tasks
                    if kind in ("PV", "PO2"):
                        done[(kind, args[0])] = tasks[0]

            def mix_ready(kk):
                if kk < HEADS // 2:
                    evacuated(*(done[("PV", hd)] for hd in (2 * kk, 2 * kk + 1)))
                elif kk < (HEADS + GRP) // 2:
                    evacuated(done["gt"][kk - HEADS // 2])
                else:
                    evacuated(*(done[("PO2", 2 * kk - HEADS - GRP + j)] for j in range(2)))

            def tiles_ready(kind, k):
                evacuated(done[(kind, k // 4)][k % 4 // 2])

            pe.wait_ge(start_in, 9 * 16)
            pe.transpose(aux_ps[:, 0, 0:2 * 58], gain_rows, ident[0:2 * 58, 0:2 * 58]).then_inc(gains_t, 1)
            pe.wait_ge(gains_in, 1)
            pe.sem_inc(s["h_ready"], N_PL)

            with pe.Fori(0, DEPTH) as layer:
                c.layer = layer
                c.n = {name: 0 for name in names}
                aux = Aux(c)
                items(-1)
                for i in range(N_IN):
                    for k in range(NG):
                        n = i * NG + k
                        if i == 0:
                            tiles_ready("T1", GK * k)
                        group(n, [GK * k, GK * k + 1], act_hi, act_lo, i, k == 0, k == NG - 1)
                        items(n)
                for i in range(N_OUT):
                    for k in range(NG):
                        n = G_OUT + i * NG + k
                        kk = k
                        if i == 0:
                            mix_ready(kk)
                        group(n, [KT + GK * kk, KT + GK * kk + 1], act_hi, act_lo, C_OUT + i,
                              k == 0, k == NG - 1)
                        items(n)

                def hidden(n0, peeled):
                    for half in range(2):
                        for k in range(NG):
                            n = n0 + half * NG + k
                            if peeled and half == 0:
                                tiles_ready("T2", GK * k)
                            group(n, [GK * k, GK * k + 1], xn_hi, xn_lo, C_FF + half, k == 0, k == NG - 1)
                            if peeled:
                                items(n)
                            elif half == 0 and k == 2:
                                HT([aux.take(b) for b in HT_BANKS])
                        ev(C_FF + half)

                hidden(G_FF, True)
                with pe.Fori(0, N_FF - 1) as i:
                    c.enter(i, PER_FF)
                    hidden(G_FF, False)
                c.leave(N_FF - 1)

                turned_last = [aux.take(b) for b in HT_BANKS]
                HT(turned_last)
                with pe.Fori(0, N_DN // 2) as i:
                    c.enter(i, PER_DN)
                    for m in range(2 * NGD):
                        k, chunk = m % NGD, C_DN + m // NGD
                        if m == 20:
                            pe.wait_ge(s["aux_free0"], turned_last[0][3])
                        if m == 21:
                            pe.wait_ge(s["aux_free1"], turned_last[1][3])
                        group(G_DN + m, [GK * k, GK * k + 1], act_hi, act_lo, chunk, k == 0, k == NGD - 1)
                        if k == NGD - 1:
                            ev(chunk)
                c.leave(N_DN // 2)
                for pair in ("pair_free0", "pair_free1"):
                    done[("down", pair)] = c.value(pair)
                evacuated(done["p"])
                for i in range(N_PJ):
                    group(G_PJ + i, [0, 1], pt_hi, pt_lo, C_PJ + i, True, True)
                    items(G_PJ + i)
                for i in range(N_PL):
                    for k in range(NG):
                        n = G_PL + i * NG + k
                        if i == 0:
                            tiles_ready("T3", GK * k)
                        group(n, [GK * k, GK * k + 1], xn_hi, xn_lo, C_PL + i, k == 0, k == NG - 1)
                        items(n)
                c.end_layer()

        @block.scalar
        def _(act):
            c = Counts(names)
            act.sem_inc(s["mm_done"], RING)
            act.dma_start(const[:], consts).then_inc(start_in, 16)
            row = 0
            for g in (norm_mix, norm_ffn, norm_ple, q_norm, k_norm, pool_scale):
                rows = g.rearrange("l (k p) -> (l k) p", p=P)
                act.dma_start(gain_rows[row:row + rows.shape[0], :], rows).then_inc(start_in, 16)
                row += rows.shape[0]
            act.dma_start(gain_rows[row:row + DEPTH * GRP, :], gmlp_b_s.rearrange("l g t -> (l g) t")
                          ).then_inc(start_in, 16)
            act.dma_start(f_bias[:], forget_bias.rearrange("l h -> (l h)").partition_broadcast(P)
                          ).then_inc(start_in, 16)
            for i in range(1, N_PL):
                cols = slice(i * COLS, (i + 1) * COLS)
                act.dma_start(h[:, :, cols], h_of(x)[:, :, cols]).then_inc(x_in[i], 16)

            def split_hi(n):
                slot = n % RING
                act.wait_ge(raw_in[slot], c.value("raw", n // RING + 1) * 16)
                act.wait_ge(s["mm_done"], c.value("mm_done", n - RING + 1))
                nc.scalar.activation(w_hi[:, slot], raw[:, slot], ACT.Copy).then_inc(s["hi_ready"], 1)

            def bank_full(task):
                act.wait_ge(s[f"aux_full{task[0]}"], task[2])
                return aux_ps[:, task[0]]

            def chunk_done(slot):
                act.wait_ge(s["mm_done"], c.value("mm_done", slot + 1))

            def answer(ins):
                ins.then_inc(s["fn_ready"], 1)
                c.add("fn_ready")

            def asked():
                c.add("arg_ready")
                act.wait_ge(s["arg_ready"], c.value("arg_ready"))

            def step(ins):
                ins.then_inc(s["act_step"], 1)
                c.add("act_step")
                act.wait_ge(s["act_step"], c.value("act_step"))

            def ev(chunk):
                c.add(f"pair_free{chunk % 2}")

            def out_of(chunk, slot, dst, func, stage):
                chunk_done(slot)
                for t in range(TB):
                    ins = nc.scalar.activation(dst[t], acc[:, chunk % 2, t, :], func, scale=rstd[:, stage, t:t + 1])
                ins.then_inc(s[f"pair_free{chunk % 2}"], 1)
                ev(chunk)

            def hi(bank, dst, gain=None):
                answer(nc.scalar.activation(dst, bank, ACT.Copy, scale=1.0 if gain is None else gain))

            def turned_h(tasks, col, dst, gain):
                for a, task in enumerate(tasks):
                    bank = bank_full(task)
                    for j in range(2):
                        k = 4 * col + 2 * a + j
                        hi(bank[:, j * SEQ:(j + 1) * SEQ], dst[:, k], lg[:, gain + k:gain + k + 1])

            def N(slot, tasks, stage):
                if stage == 0:
                    for q in x_in:
                        act.wait_ge(q, 16)
                    act.wait_ge(s["h_ready"], c.value("h_ready", 0))
                else:
                    for pair in ("pair_free0", "pair_free1"):
                        act.wait_ge(s[pair], c.value(pair))
                flat = scratch[:].rearrange("p t n -> p (t n)")
                for i in range(2 * TB):
                    t, half = divmod(i, 2)
                    ins = nc.scalar.activation(flat, h[:, t, half * D // 2:(half + 1) * D // 2], ACT.Square,
                                               accum_out=ssq[:, i:i + 1])
                    if i < 2 * TB - 1:
                        step(ins)
                answer(ins)
                asked()
                answer(nc.scalar.activation(dev, var, ACT.Sqrt))
                asked()

            def NRM(slot, tasks, *_):
                asked()
                answer(nc.scalar.activation(hdev, hvar, ACT.Sqrt))

            def EVQK(slot, tasks, chunk, half, which):
                if half or which:
                    for t in last_qk:
                        act.wait_ge(s[f"aux_free{t[0]}"], t[3])
                out_of(chunk, slot, [qk_nat[:, t] for t in range(TB)], ACT.Copy, 0)

            last_qk = []

            def TQK(slot, tasks, half, which):
                last_qk[:] = tasks

            def EVV(slot, tasks, chunk, half):
                out_of(chunk, slot, [v_nat[:, half, t] for t in range(TB)], ACT.Copy, 0)

            def EVXP(slot, tasks, chunk):
                out_of(chunk, slot, [xp[:, t] for t in range(TB)], ACT.Copy, 0)

            def flat_of(x4):
                return [x4[:, t].rearrange("p g c -> p (g c)") for t in range(TB)]

            def EVGU(slot, tasks, chunk):
                out_of(chunk, slot, flat_of(gu), ACT.Gelu_apprx_tanh, 0)

            def EVGV(slot, tasks, chunk):
                out_of(chunk, slot, flat_of(gv), ACT.Gelu_apprx_tanh, 0)

            def WF(slot, tasks):
                act.wait_ge(s["wf_in"], c.value("wf_in", PER_LAYER["wf_in"]))
                answer(nc.scalar.activation(wf_hi, wf[:], ACT.Copy))

            def FX(slot, tasks):
                asked()
                step(nc.scalar.activation(ef, nz, ACT.Exp))
                answer(nc.scalar.activation(lnf, ef, ACT.Ln, bias=1.0))

            def C(slot, tasks):
                answer(nc.scalar.activation(neg_cum[0:HEADS], bank_full(tasks[0])[0:HEADS, P:P + SEQ], ACT.Copy,
                                            scale=-1.0))

            def SX(slot, tasks, hd):
                asked()
                pr = work[:, hd % 2].rearrange("p (t k) -> p t k", t=TB)
                for t, keys in ((0, P), (1, SEQ)):
                    ins = nc.scalar.activation(pr[:, t, 0:keys], pr[:, t, 0:keys], ACT.Exp,
                                               bias=nmx[:, t:t + 1], accum_out=den[:, t:t + 1])
                answer(ins)

            def PT(slot, tasks, hd):
                bank = bank_full(tasks[0])
                nc.scalar.activation(probs_t[:, hd % 2], bank[:, 0:3 * P], ACT.Copy
                                     ).then_inc(s[f"aux_free{tasks[0][0]}"], 1)

            def PV(slot, tasks, hd):
                hi(bank_full(tasks[0])[:, 0:SEQ], act_hi[:, KT + hd])

            def PT_P(slot, tasks):
                hi(bank_full(tasks[0])[:], pt_hi[:].rearrange("p k t -> p (k t)"))

            def PO1(slot, tasks, g):
                bank = bank_full(tasks[0])
                nc.scalar.activation(pool_d[:, g], bank[:, 0:SEQ], ACT.Copy).then_inc(s[f"aux_free{tasks[0][0]}"], 1)

            def PO2(slot, tasks, g):
                hi(bank_full(tasks[0])[:, 0:SEQ], act_hi[:, KT + HEADS + GRP + g], lg[:, 50 + g:51 + g])

            def GT(slot, tasks):
                for a, task in enumerate(tasks):
                    k = KT + HEADS + 2 * a
                    hi(bank_full(task)[:], act_hi[:, k:k + 2].rearrange("p k t -> p (k t)"))

            def T1(slot, tasks, col):
                turned_h(tasks, col, act_hi, 0)

            def T2(slot, tasks, col):
                turned_h(tasks, col, xn_hi, KT)

            def T3(slot, tasks, col):
                turned_h(tasks, col, xn_hi, 2 * KT)

            def EVOUT(slot, tasks, chunk, col):
                ev(chunk)

            def EVPJ(slot, tasks, chunk, col):
                chunk_done(slot)
                nc.scalar.activation(ple[:, col], acc[:, chunk % 2], ACT.Copy
                                     ).then_inc(s[f"pair_free{chunk % 2}"], 1)
                ev(chunk)

            def EVPL(slot, tasks, chunk, col):
                act.wait_ge(s["h_ready"], c.value("h_ready"))
                out_of(chunk, slot, [scratch[:, t] for t in range(TB)], ACT.Sigmoid, 2)
                c.add("h_ready")

            def nothing(slot, tasks, *_):
                pass

            do = {"T1": T1, "T2": T2, "T3": T3, "TQK": TQK, "FM": nothing, "FT": nothing, "C": C,
                  "S": nothing, "SX": SX, "NRM": NRM, "FX": FX, "PT": PT, "PV": PV, "PT_P": PT_P,
                  "PO1": PO1, "PO2": PO2, "WS": nothing, "GM": nothing, "GT": GT, "EVQK": EVQK, "EVV": EVV,
                  "EVXP": EVXP, "EVGU": EVGU, "EVGV": EVGV, "EVOUT": EVOUT, "EVPJ": EVPJ,
                  "EVPL": EVPL, "N": N, "WF": WF, "F": nothing}

            def items(slot):
                for kind, *args in PLAN.get(slot, ()):
                    do[kind](slot, [aux.take() for _ in range(TASKS[kind])], *args)

            def run(first, end):
                for n in range(first, end):
                    if n + LEAD < GROUPS:
                        split_hi(n + LEAD)
                    items(n)

            def HT(tasks, k, register=None):
                for a, task in enumerate(tasks):
                    bank = bank_full(task)
                    first = k + 2 * a if register is None else register * 4 + (k + 2 * a)
                    hi(bank, act_hi[:, bass.ds(first, 2)].rearrange("p k t -> p (k t)"))

            def hidden(n0, register):
                for j in range(2 * NG):
                    n = n0 + j
                    split_hi(n + LEAD)
                    if register is None:
                        items(n)
                    elif j == 2:
                        HT([aux.take(b) for b in HT_BANKS], 0, register)
                    if j == NG - 1:
                        act.wait_ge(s[f"pair_free{(C_FF + 1) % 2}"], c.value(f"pair_free{(C_FF + 1) % 2}"))
                        out_of(C_FF, n, [scratch[:, t] for t in range(TB)], ACT.Silu, 1)
                    if j == 2 * NG - 1:
                        ev(C_FF + 1)

            with act.Fori(0, DEPTH) as layer:
                c.layer, c.n = layer, {name: 0 for name in names}
                aux = Aux(c)
                split_hi(0)
                act.wait_ge(s["layer_start"], layer + 1)
                items(-1)
                for n in range(1, LEAD):
                    split_hi(n)
                run(0, G_FF)
                hidden(G_FF, None)
                with act.Fori(0, N_FF - 1) as i:
                    c.enter(i, PER_FF)
                    hidden(G_FF + 2 * NG, i)
                c.leave(N_FF - 1)
                HT([aux.take(b) for b in HT_BANKS], 4 * (N_FF - 1))
                with act.Fori(0, N_DN // 2) as i:
                    c.enter(i, PER_DN)
                    for m in range(2 * NGD):
                        split_hi(G_DN + m + LEAD)
                        if m % NGD == NGD - 1:
                            ev(C_DN + m // NGD)
                c.leave(N_DN // 2)
                run(G_PJ, GROUPS)
                c.end_layer()

        @block.vector
        def _(dve):
            c = Counts(names)

            def split_lo(n):
                slot = n % RING
                dve.wait_ge(s["hi_ready"], c.value("hi_ready", n + 1))
                nc.vector.tensor_tensor(w_lo[:, slot], raw[:, slot], w_hi[:, slot].bitcast(F32), ALU.subtract
                                        ).then_inc(s["lo_ready"], 1)

            def bank_full(task):
                dve.wait_ge(s[f"aux_full{task[0]}"], task[2])
                return aux_ps[:, task[0]]

            def free(ins, task):
                ins.then_inc(s[f"aux_free{task[0]}"], 1)

            def chunk_done(slot):
                dve.wait_ge(s["mm_done"], c.value("mm_done", slot + 1))

            def step(ins):
                ins.then_inc(s["dve_step"], 1)
                c.add("dve_step")
                dve.wait_ge(s["dve_step"], c.value("dve_step"))

            def ask(ins):
                ins.then_inc(s["arg_ready"], 1)
                c.add("arg_ready")

            def answered(k=1):
                c.add("fn_ready", k)
                dve.wait_ge(s["fn_ready"], c.value("fn_ready"))

            def ev(chunk):
                c.add(f"pair_free{chunk % 2}")

            def pair_out(chunk):
                ev(chunk)
                dve.wait_ge(s[f"pair_free{chunk % 2}"], c.value(f"pair_free{chunk % 2}"))

            def lo(bank, dst_hi, dst, gain=None):
                if gain is None:
                    answered()
                    return nc.vector.tensor_tensor(dst, bank, dst_hi.bitcast(F32), ALU.subtract)
                return nc.vector.scalar_tensor_tensor(out=dst, in0=bank, scalar=gain, in1=dst_hi.bitcast(F32),
                                                      op0=ALU.mult, op1=ALU.subtract)

            def turned_h(tasks, col, dst_hi, dst, gain):
                for a, task in enumerate(tasks):
                    bank = bank_full(task)
                    answered(2)
                    for j in range(2):
                        k = 4 * col + 2 * a + j
                        ins = lo(bank[:, j * SEQ:(j + 1) * SEQ], dst_hi[:, k], dst[:, k],
                                 lg[:, gain + k:gain + k + 1])
                    free(ins, task)

            def N(slot, tasks, stage):
                answered()
                step(nc.vector.tensor_tensor(var, ssq[:, 0:4:2], ssq[:, 1:4:2], ALU.add))
                ask(nc.vector.tensor_scalar(var, var, 1.0 / D, EPS, ALU.mult, ALU.add))
                answered()
                ask(nc.vector.reciprocal(rstd[:, stage], dev))

            def head_squares(x3):
                sq = scratch[:].rearrange("p t (g c) -> p (t g) c", c=P)
                step(nc.vector.tensor_tensor(sq, x3, x3, ALU.mult))
                step(nc.vector.tensor_reduce(hss, sq, AX_X, ALU.add))
                ask(nc.vector.tensor_scalar(hvar, hss, 1.0 / HD, EPS, ALU.mult, ALU.add))

            def NRM(slot, tasks, gated=False):
                x3, gain = qk_nat[:].rearrange("p t (g c) -> p (t g) c", c=P), None
                if gated:
                    x3, gain = gv[:].rearrange("p t g c -> p (t g) c"), v_gain[:]
                answered()
                step(nc.vector.reciprocal(hr, hdev))
                ins = nc.vector.tensor_tensor(x3, x3, hr.unsqueeze(2).to_broadcast([P, TB * GRP, P]), ALU.mult)
                if gain is not None:
                    step(ins)
                    x = x3.rearrange("p (t g) c -> p t (g c)", t=TB)
                    ins = nc.vector.tensor_tensor(x, x, gain.unsqueeze(1).to_broadcast([P, TB, MIXW]), ALU.mult)
                ins.then_inc(s["norm_ready"], 1)
                c.add("norm_ready")

            def EVQK(slot, tasks, chunk, half, which):
                pair_out(chunk)
                head_squares(qk_nat[:].rearrange("p t (g c) -> p (t g) c", c=P))

            def EVGV(slot, tasks, chunk):
                pair_out(chunk)
                head_squares(gv[:].rearrange("p t g c -> p (t g) c"))

            def TQK(slot, tasks, half, which):
                dst = (q_t, k_t)[which]
                for a, task in enumerate(tasks):
                    bank = bank_full(task)
                    free(nc.vector.tensor_scalar(dst[:, half, 2 * a:2 * a + 2].rearrange("p h t -> p (h t)"), bank,
                                                 lg[:, 48 + which:49 + which], (SCALE, 1.0)[which],
                                                 ALU.mult, ALU.mult), task)

            def WF(slot, tasks):
                answered()
                nc.vector.tensor_tensor(wf_lo, wf[:], wf_hi.bitcast(F32), ALU.subtract
                                        ).then_inc(s["wf_ready"], 1)

            def FM(slot, tasks):
                free(nc.vector.tensor_copy(f_rows, bank_full(tasks[0])[0:2 * HEADS, 0:SEQ]), tasks[0])

            def FT(slot, tasks):
                forget[:] = tasks

            def F(slot, tasks):
                (task,) = forget
                bank = bank_full(task)
                step(nc.vector.tensor_reduce(
                    fsum, bank[:, 0:TB * 2 * HEADS].rearrange("p (t a h) -> p t h a", t=TB, a=2), AX_X, ALU.add))
                for t in range(TB):
                    ins = nc.vector.scalar_tensor_tensor(out=z[:, t], in0=fsum[:, t], scalar=rstd[:, 0, t:t + 1],
                                                         in1=lf_bias[:], op0=ALU.mult, op1=ALU.add)
                free(ins, task)
                dve.wait_ge(s[f"aux_free{task[0]}"], task[3])
                step(nc.vector.tensor_scalar(nz, z, -1.0, None, ALU.mult))
                ask(nc.vector.tensor_tensor(nz, nz, z, ALU.min))

            def FX(slot, tasks):
                step(nc.vector.tensor_scalar(logf, z, 0.0, None, ALU.min))
                answered()
                nc.vector.tensor_tensor(logf, logf, lnf, ALU.subtract).then_inc(s["gates_ready"], 1)
                c.add("gates_ready")

            def C(slot, tasks):
                bank = bank_full(tasks[0])
                answered()
                step(nc.vector.tensor_copy(cum, bank[:, 0:TB * HEADS].rearrange("p (t h) -> p t h", t=TB)))
                free(nc.vector.scalar_tensor_tensor(
                    out=neg_cum[LO_ROW:LO_ROW + HEADS], in0=bank[0:HEADS, P:P + SEQ], scalar=-1.0,
                    in1=neg_cum[0:HEADS].bitcast(F32), op0=ALU.mult, op1=ALU.subtract), tasks[0])

            def S(slot, tasks, hd):
                bank = bank_full(tasks[0])
                pr = work[:, hd % 2].rearrange("p (t k) -> p t k", t=TB)
                for t, keys in ((0, P), (1, SEQ)):
                    ins = nc.vector.scalar_tensor_tensor(
                        out=pr[:, t, 0:keys], in0=bank[:, t * SEQ:t * SEQ + keys], scalar=cum[:, t, hd:hd + 1],
                        in1=mask[:, SEQ - keys:SEQ], op0=ALU.add, op1=ALU.add)
                free(ins, tasks[0])
                dve.wait_ge(s[f"aux_free{tasks[0][0]}"], tasks[0][3])
                nc.vector.tensor_reduce(mx[:, 0:1], pr[:, 0, 0:P], AX_X, ALU.max)
                step(nc.vector.tensor_reduce(mx[:, 1:2], pr[:, 1], AX_X, ALU.max))
                ask(nc.vector.tensor_scalar(nmx, mx, -1.0, None, ALU.mult))

            def SX(slot, tasks, hd):
                pr = work[:, hd % 2].rearrange("p (t k) -> p t k", t=TB)
                answered()
                step(nc.vector.reciprocal(rden, den))
                for t, keys in ((0, P), (1, SEQ)):
                    ins = nc.vector.tensor_scalar(pr[:, t, 0:keys], pr[:, t, 0:keys], rden[:, t:t + 1], None, ALU.mult)
                ins.then_inc(s["probs_ready"], 1)
                c.add("probs_ready")

            def PV(slot, tasks, hd):
                bank = bank_full(tasks[0])
                free(lo(bank[:, 0:SEQ], act_hi[:, KT + hd], act_lo[:, KT + hd]), tasks[0])

            def PT_P(slot, tasks):
                bank = bank_full(tasks[0])
                free(lo(bank, pt_hi[:].rearrange("p k t -> p (k t)"), pt_lo[:].rearrange("p k t -> p (k t)")), tasks[0])

            def PO2(slot, tasks, g):
                bank = bank_full(tasks[0])
                k = KT + HEADS + GRP + g
                answered()
                free(lo(bank[:, 0:SEQ], act_hi[:, k], act_lo[:, k], lg[:, 50 + g:51 + g]), tasks[0])

            def WS(slot, tasks):
                bank = bank_full(tasks[0])
                free(nc.vector.tensor_tensor(w_st[:], bank.rearrange("p (g t) -> p g t", g=GRP),
                                             upper.unsqueeze(1).to_broadcast([P, GRP, P]), ALU.mult), tasks[0])

            def GM(slot, tasks):
                for t, task in enumerate(tasks):
                    bank = bank_full(task)
                    for g in range(GRP):
                        ins = nc.vector.scalar_tensor_tensor(
                            out=gu[:, t, g], in0=bank[:, g * P:(g + 1) * P], scalar=lg[:, 54 + g:55 + g],
                            in1=gu[:, t, g], op0=ALU.add, op1=ALU.mult)
                    free(ins, task)

            def GT(slot, tasks):
                for a, task in enumerate(tasks):
                    bank = bank_full(task)
                    k = KT + HEADS + 2 * a
                    free(lo(bank, act_hi[:, k:k + 2].rearrange("p k t -> p (k t)"),
                            act_lo[:, k:k + 2].rearrange("p k t -> p (k t)")), task)

            def T1(slot, tasks, col):
                turned_h(tasks, col, act_hi, act_lo, 0)

            def T2(slot, tasks, col):
                turned_h(tasks, col, xn_hi, xn_lo, KT)

            def T3(slot, tasks, col):
                turned_h(tasks, col, xn_hi, xn_lo, 2 * KT)

            def add_to_h(chunk, n, cols):
                chunk_done(n)
                nc.vector.tensor_tensor(h[:, :, cols], h[:, :, cols], acc[:, chunk % 2], ALU.add
                                        ).then_inc(s[f"pair_free{chunk % 2}"], 1)
                ev(chunk)

            def EVOUT(slot, tasks, chunk, col):
                add_to_h(chunk, slot, slice(col * COLS, (col + 1) * COLS))

            def EVPL(slot, tasks, chunk, col):
                pair_out(chunk)
                cols = slice(col * COLS, (col + 1) * COLS)
                step(nc.vector.tensor_tensor(work[:], scratch[:], ple[:, col], ALU.mult))
                nc.vector.tensor_tensor(h[:, :, cols], h[:, :, cols], work[:], ALU.add).then_inc(s["h_ready"], 1)
                c.add("h_ready")

            def counted(slot, tasks, chunk, *_):
                ev(chunk)

            def nothing(slot, tasks, *_):
                pass

            do = {"T1": T1, "T2": T2, "T3": T3, "TQK": TQK, "FM": FM, "FT": FT, "C": C, "S": S,
                  "PT": nothing, "PV": PV, "PT_P": PT_P,
                  "PO1": nothing, "PO2": PO2, "WS": WS, "GM": GM, "GT": GT, "EVQK": EVQK, "EVV": counted,
                  "EVXP": counted, "EVGU": counted, "EVGV": EVGV, "EVOUT": EVOUT, "EVPJ": counted,
                  "EVPL": EVPL, "N": N, "WF": WF, "F": F, "NRM": NRM, "SX": SX, "FX": FX}

            def items(slot):
                for kind, *args in PLAN.get(slot, ()):
                    do[kind](slot, [aux.take() for _ in range(TASKS[kind])], *args)

            forget = []

            def run(first, end):
                for n in range(first, end):
                    if n + LEAD < GROUPS:
                        split_lo(n + LEAD)
                    items(n)

            def HT(tasks, k, register=None):
                for a, task in enumerate(tasks):
                    bank = bank_full(task)
                    first = k + 2 * a if register is None else register * 4 + (k + 2 * a)
                    free(lo(bank, act_hi[:, bass.ds(first, 2)].rearrange("p k t -> p (k t)"),
                            act_lo[:, bass.ds(first, 2)].rearrange("p k t -> p (k t)")), task)

            def hidden(n0, register):
                for j in range(2 * NG):
                    n = n0 + j
                    split_lo(n + LEAD)
                    if register is None:
                        items(n)
                    elif j == 2:
                        HT([aux.take(b) for b in HT_BANKS], 0, register)
                    if j == NG - 1:
                        ev(C_FF)
                    if j == 2 * NG - 1:
                        gate = f"pair_free{C_FF % 2}"
                        dve.wait_ge(s[gate], c.value(gate))
                        chunk_done(n)
                        for t in range(TB):
                            ins = nc.vector.scalar_tensor_tensor(
                                out=work[:, t], in0=acc[:, (C_FF + 1) % 2, t], scalar=rstd[:, 1, t:t + 1],
                                in1=scratch[:, t], op0=ALU.mult, op1=ALU.mult)
                        ins.then_inc(s[f"pair_free{(C_FF + 1) % 2}"], 1)
                        ev(C_FF + 1)

            dve.wait_ge(gains_t, 1)
            nc.vector.tensor_copy(gains[:], aux_ps[:, 0, 0:2 * 58]).then_inc(gains_in, 1)
            dve.wait_ge(gains_in, 1)
            nc.vector.memset(neg_cum[:].bitcast(mybir.dt.uint32), 0)
            nc.vector.tensor_copy(both[:], both_rows)
            with dve.Fori(0, DEPTH) as layer:
                c.layer, c.n = layer, {name: 0 for name in names}
                aux = Aux(c)
                nc.vector.tensor_copy(lf_bias[:], f_bias[:, bass.ds(layer * HEADS, HEADS)])
                for col, kinds, each in ((0, 3, KT), (48, 2, 1), (50, 2, GRP)):
                    src = gains[:, 2 * col:2 * (col + kinds * each)].rearrange("p (s l k) -> p s l k", l=DEPTH, k=each)
                    ins = nc.vector.tensor_copy(
                        lg[:, col:col + kinds * each].rearrange("p (s k) -> p s k", k=each),
                        src[:, :, bass.ds(layer, 1)].rearrange("p s l k -> p s (l k)"))
                ins.then_inc(s["layer_start"], 1)
                dve.wait_ge(s["layer_start"], layer + 1)
                split_lo(0)
                items(-1)
                for n in range(1, LEAD):
                    split_lo(n)
                run(0, G_FF)
                hidden(G_FF, None)
                with dve.Fori(0, N_FF - 1) as i:
                    c.enter(i, PER_FF)
                    hidden(G_FF + 2 * NG, i)
                c.leave(N_FF - 1)
                HT([aux.take(b) for b in HT_BANKS], 4 * (N_FF - 1))
                with dve.Fori(0, N_DN // 2) as i:
                    c.enter(i, PER_DN)
                    for m in range(2 * NGD):
                        split_lo(G_DN + m + LEAD)
                        if m % NGD == NGD - 1:
                            add_to_h(C_DN + m // NGD, G_DN + m, bass.ds(i * (2 * COLS) + m // NGD * COLS, COLS))
                c.leave(N_DN // 2)
                run(G_PJ, GROUPS)
                c.end_layer()


_INS = ["x", "p", "norm_mix", "w_in", "q_norm", "k_norm", "forget_bias", "gmlp_v_norm", "gmlp_w_s", "gmlp_b_s",
        "pool_w", "pool_scale", "w_out", "norm_ffn", "w_ffn_gate", "w_ffn_up", "w_ffn_down", "norm_ple",
        "w_ple_gate", "w_ple_proj"]


def shape_constants():
    i = np.arange(P)
    upper = (i[:, None] <= i[None, :]).astype(np.float32)
    mask = np.where(i[None, :] <= i[:, None], 0.0, MASKED).astype(np.float32)
    both = np.zeros((P, HEADS), np.float32)
    both[:HEADS] = both[LO_ROW:LO_ROW + HEADS] = np.eye(HEADS)
    consts = np.concatenate([np.eye(P, dtype=np.float32), upper, np.ones((P, P), np.float32),
                             np.zeros((P, P), np.float32), mask, both], axis=1)
    t = np.arange(SEQ)
    bands = np.zeros((P, GRP, 3, P), np.float32)
    for g, win in enumerate(WINDOWS):
        count = np.minimum(t + 1, win).astype(np.float32)
        inside = (t[:, None] <= t[None, :]) & (t[:, None] > t[None, :] - win)
        full = (inside / count[None, :] - np.eye(SEQ)).astype(np.float32)
        bands[:, g, 0], bands[:, g, 1], bands[:, g, 2] = full[:P, :P], full[:P, P:], full[P:, P:]
    return consts, bands


def kernel(**inputs):
    import concourse.bacc as _bacc
    from concourse.bass_utils import run_bass_kernel_spmd as _run

    nc = _bacc.Bacc("TRN2", target_bir_lowering=False, num_devices=1)
    consts, bands = shape_constants()
    arrays, args = {}, []
    for name, a in [(n, inputs[n]) for n in _INS] + [("consts", consts), ("bands", bands)]:
        a = np.ascontiguousarray(a)
        arrays[f"in_{name}_dram"] = a
        args.append(nc.dram_tensor(f"in_{name}_dram", a.shape, mybir.dt.from_np(a.dtype), kind="ExternalInput").ap())
    args.append(nc.dram_tensor("out_0_dram", (1, SEQ, D), F32, kind="ExternalOutput").ap())
    trunk(nc, *args)
    r = _run(nc, [arrays], core_ids=[0])
    return r.results[0]["out_0_dram"]
```
